# Optimizing a Trainium2 kernel written in Bass

```python
import jax, jax.numpy as jnp
from jax import lax
import numpy as np
import math

D_MODEL = 1024
BATCH = 1
SEQ = 512
DEPTH = 2

CHUNK = 64
BRANCH_W = 512
N_BRANCH = 3
EPS = 1e-6
SG_BLOCK = 128
SG_GROUPS = 4
SG_GROUP_W = BRANCH_W // SG_GROUPS
MLA_HEADS = 8
MLA_NOPE = 64
MLA_ROPE = 32
MLA_QK = MLA_NOPE + MLA_ROPE
MLA_V = 64
MLA_Q_RANK = 256
MLA_KV_RANK = 128
ROPE_THETA = 10000.0
Q_BLOCK = 128
GLA_HEADS = 4
GLA_DK = 64
GLA_DV = 128
GLA_GATE_RANK = 16
GLA_TAU = 16.0

SPLITS = (BRANCH_W, BRANCH_W, BRANCH_W,
          MLA_Q_RANK, MLA_KV_RANK, MLA_ROPE, MLA_HEADS * MLA_V,
          GLA_HEADS * GLA_DK, GLA_HEADS * GLA_DK, GLA_HEADS * GLA_DV,
          GLA_GATE_RANK, GLA_HEADS * GLA_DV,
          N_BRANCH * D_MODEL)
IN_COLS = sum(SPLITS)


def _rmsnorm(x, g):
    x32 = x.astype(jnp.float32)
    y = x32 * lax.rsqrt(jnp.mean(x32 * x32, axis=-1, keepdims=True) + EPS)
    return (y * g.astype(jnp.float32)).astype(x.dtype)

def _layernorm(x, g, b):
    x32 = x.astype(jnp.float32)
    mu = jnp.mean(x32, axis=-1, keepdims=True)
    xc = x32 - mu
    y = xc * lax.rsqrt(jnp.mean(xc * xc, axis=-1, keepdims=True) + EPS)
    return (y * g.astype(jnp.float32) + b.astype(jnp.float32)).astype(x.dtype)

def _split_cols(proj):
    idx = np.cumsum(np.array(SPLITS))[:-1].tolist()
    return jnp.split(proj, idx, axis=-1)

def _rope_tables(positions):
    half = MLA_ROPE // 2
    inv = 1.0 / (ROPE_THETA ** (jnp.arange(half, dtype=jnp.float32) * 2.0 / MLA_ROPE))
    ang = positions.astype(jnp.float32)[..., None] * inv
    return jnp.cos(ang)[:, :, None, :], jnp.sin(ang)[:, :, None, :]

def _apply_rope(x, cos, sin):
    half = MLA_ROPE // 2
    x32 = x.astype(jnp.float32)
    x1, x2 = x32[..., :half], x32[..., half:]
    return jnp.concatenate([x1 * cos - x2 * sin, x1 * sin + x2 * cos], axis=-1).astype(x.dtype)

def _spatial_gating(u, v, z, ln_g, ln_b, w_s, b_s):
    bn, s, _ = u.shape
    u = jax.nn.gelu(u)
    v = _layernorm(jax.nn.gelu(v), ln_g, ln_b)
    nb = s // SG_BLOCK
    vb = v.reshape(bn, nb, SG_BLOCK, SG_GROUPS, SG_GROUP_W)
    cid = jnp.arange(SG_BLOCK) // CHUNK
    mask = cid[:, None] >= cid[None, :]
    w = jnp.where(mask[None], w_s, jnp.zeros_like(w_s))
    sv = jnp.einsum('gij,bnjgc->bnigc', w, vb) + b_s.T[None, None, :, :, None]
    return u * sv.reshape(bn, s, BRANCH_W) * jax.nn.silu(z)

def _chunk_causal_attention(q, k, v):
    bn, s, h, dq = q.shape
    dv = v.shape[-1]
    nb = s // Q_BLOCK
    scale = dq ** -0.5
    qb = q.reshape(bn, nb, Q_BLOCK, h, dq).transpose(1, 0, 3, 2, 4)
    kh = k.transpose(0, 2, 1, 3)
    vh = v.transpose(0, 2, 1, 3)
    k_chunk = jnp.arange(s) // CHUNK

    def one_block(args):
        qblk, bi = args
        sc = jnp.einsum('bhqd,bhkd->bhqk', qblk, kh).astype(jnp.float32) * scale
        q_chunk = (bi * Q_BLOCK + jnp.arange(Q_BLOCK)) // CHUNK
        mask = k_chunk[None, :] <= q_chunk[:, None]
        sc = jnp.where(mask, sc, -jnp.inf)
        p = jax.nn.softmax(sc, axis=-1)
        return jnp.einsum('bhqk,bhkd->bhqd', p.astype(vh.dtype), vh)

    out = lax.map(one_block, (qb, jnp.arange(nb)))
    return out.transpose(1, 0, 3, 2, 4).reshape(bn, s, h, dv)

def _mla(c_q, c_kv, k_r, z, cq_g, ckv_g, w_uq, w_ukv, q_g, k_g, cos, sin):
    bn, s, _ = c_q.shape
    q = (_rmsnorm(c_q, cq_g) @ w_uq).reshape(bn, s, MLA_HEADS, MLA_QK)
    kv = (_rmsnorm(c_kv, ckv_g) @ w_ukv).reshape(bn, s, MLA_HEADS, MLA_NOPE + MLA_V)
    k_nope, v = kv[..., :MLA_NOPE], kv[..., MLA_NOPE:]
    k_rope = jnp.broadcast_to(k_r[:, :, None, :], (bn, s, MLA_HEADS, MLA_ROPE))
    k = jnp.concatenate([k_nope, k_rope], axis=-1)
    q = _rmsnorm(q, q_g)
    k = _rmsnorm(k, k_g)
    q = jnp.concatenate([q[..., :MLA_NOPE], _apply_rope(q[..., MLA_NOPE:], cos, sin)], axis=-1)
    k = jnp.concatenate([k[..., :MLA_NOPE], _apply_rope(k[..., MLA_NOPE:], cos, sin)], axis=-1)
    o = _chunk_causal_attention(q, k, v)
    return o.reshape(bn, s, MLA_HEADS * MLA_V) * jax.nn.silu(z)

def _gla(q, k, v, g_lr, z, w_gu, b_gu, o_g):
    bn, s, _ = q.shape
    n = s // CHUNK
    f32 = jnp.float32
    qc = q.astype(f32).reshape(bn, n, CHUNK, GLA_HEADS, GLA_DK) * (GLA_DK ** -0.5)
    kc = k.astype(f32).reshape(bn, n, CHUNK, GLA_HEADS, GLA_DK)
    vc = v.astype(f32).reshape(bn, n, CHUNK, GLA_HEADS, GLA_DV)
    log_a = jax.nn.log_sigmoid((g_lr @ w_gu + b_gu).astype(f32)) / GLA_TAU
    log_a = log_a.reshape(bn, n, CHUNK, GLA_HEADS, GLA_DK)
    b = jnp.cumsum(log_a, axis=2)
    b_last = b[:, :, -1]
    q_t = qc * jnp.exp(b)
    k_t = kc * jnp.exp(-b)
    k_s = kc * jnp.exp(b_last[:, :, None] - b)
    causal = jnp.tril(jnp.ones((CHUNK, CHUNK), dtype=bool))
    att = jnp.einsum('bnihd,bnjhd->bnhij', q_t, k_t)
    att = jnp.where(causal, att, 0.0)
    o_intra = jnp.einsum('bnhij,bnjhe->bnihe', att, vc)

    def step(state, xs):
        q_i, k_i, v_i, dec = xs
        o_i = jnp.einsum('bihd,bhde->bihe', q_i, state)
        new_state = dec[..., None] * state + jnp.einsum('bjhd,bjhe->bhde', k_i, v_i)
        return new_state, o_i

    s0 = jnp.zeros((bn, GLA_HEADS, GLA_DK, GLA_DV), f32)
    xs = (jnp.moveaxis(q_t, 1, 0), jnp.moveaxis(k_s, 1, 0), jnp.moveaxis(vc, 1, 0), jnp.moveaxis(jnp.exp(b_last), 1, 0))
    _, o_inter = lax.scan(step, s0, xs)
    o = (o_intra + jnp.moveaxis(o_inter, 0, 1)).reshape(bn, s, GLA_HEADS, GLA_DV)
    o = _rmsnorm(o, o_g).reshape(bn, s, GLA_HEADS * GLA_DV).astype(z.dtype)
    return o * jax.nn.silu(z)

def first_inputs(seed: int = 0) -> dict:
    key = jax.random.key(seed)
    ks = jax.random.split(key, 24)
    f32 = jnp.float32
    nrm = lambda k, shp, sc: jax.random.normal(k, shp, f32) * sc
    gain = lambda k, shp: 1.0 + 0.02 * jax.random.normal(k, shp, f32)
    x = jax.random.normal(ks[0], (BATCH, SEQ, D_MODEL), f32)
    offset = jax.random.randint(ks[1], (BATCH, 1), 0, 4096, dtype=jnp.int32)
    positions = offset + jnp.arange(SEQ, dtype=jnp.int32)[None, :]
    return {
        'x': x,
        'positions': positions,
        'norm_g': gain(ks[2], (DEPTH, D_MODEL)),
        'w_in': nrm(ks[3], (DEPTH, D_MODEL, IN_COLS), D_MODEL ** -0.5),
        'b_gate': nrm(ks[4], (DEPTH, N_BRANCH * D_MODEL), 0.1),
        'sg_ln_g': gain(ks[5], (DEPTH, BRANCH_W)),
        'sg_ln_b': nrm(ks[6], (DEPTH, BRANCH_W), 0.02),
        'sg_w': nrm(ks[7], (DEPTH, SG_GROUPS, SG_BLOCK, SG_BLOCK), SG_BLOCK ** -0.5),
        'sg_b': gain(ks[8], (DEPTH, SG_GROUPS, SG_BLOCK)),
        'mla_cq_g': gain(ks[9], (DEPTH, MLA_Q_RANK)),
        'mla_ckv_g': gain(ks[10], (DEPTH, MLA_KV_RANK)),
        'mla_w_uq': nrm(ks[11], (DEPTH, MLA_Q_RANK, MLA_HEADS * MLA_QK), MLA_Q_RANK ** -0.5),
        'mla_w_ukv': nrm(ks[12], (DEPTH, MLA_KV_RANK, MLA_HEADS * (MLA_NOPE + MLA_V)), MLA_KV_RANK ** -0.5),
        'mla_q_g': gain(ks[13], (DEPTH, MLA_QK)),
        'mla_k_g': gain(ks[14], (DEPTH, MLA_QK)),
        'gla_w_gate': nrm(ks[15], (DEPTH, GLA_GATE_RANK, GLA_HEADS * GLA_DK), GLA_GATE_RANK ** -0.5),
        'gla_b_gate': nrm(ks[16], (DEPTH, GLA_HEADS * GLA_DK), 0.1),
        'gla_o_g': gain(ks[17], (DEPTH, GLA_DV)),
        'w_branch': nrm(ks[18], (DEPTH, N_BRANCH, BRANCH_W, D_MODEL), BRANCH_W ** -0.5),
        'w_out': nrm(ks[19], (DEPTH, D_MODEL, D_MODEL), D_MODEL ** -0.5),
    }

def first_block(x, positions, norm_g, w_in, b_gate, sg_ln_g, sg_ln_b, sg_w, sg_b, mla_cq_g, mla_ckv_g,
              mla_w_uq, mla_w_ukv, mla_q_g, mla_k_g, gla_w_gate, gla_b_gate, gla_o_g, w_branch, w_out):
    bn, s, d = x.shape
    cos, sin = _rope_tables(positions)
    for l in range(DEPTH):
        h = _rmsnorm(x, norm_g[l])
        (u_a, v_a, z_a, c_q, c_kv, k_r, z_b, q_c, k_c, v_c, g_c, z_c, gate_logits) = _split_cols(h @ w_in[l])
        y_a = _spatial_gating(u_a, v_a, z_a, sg_ln_g[l], sg_ln_b[l], sg_w[l], sg_b[l])
        y_b = _mla(c_q, c_kv, k_r, z_b, mla_cq_g[l], mla_ckv_g[l], mla_w_uq[l], mla_w_ukv[l],
                   mla_q_g[l], mla_k_g[l], cos, sin)
        y_c = _gla(q_c, k_c, v_c, g_c, z_c, gla_w_gate[l], gla_b_gate[l], gla_o_g[l])
        gates = jax.nn.sigmoid(gate_logits + b_gate[l]).reshape(bn, s, N_BRANCH, d)
        merged = (gates[:, :, 0] * (y_a @ w_branch[l, 0])
                  + gates[:, :, 1] * (y_b @ w_branch[l, 1])
                  + gates[:, :, 2] * (y_c @ w_branch[l, 2]))
        x = x + merged @ w_out[l]
    return x


HEAD_DIM = 64
N_HEADS_MOBA = 6
N_HEADS_DIL = 6
N_HEADS_MEM = 4
D_MOBA = N_HEADS_MOBA * HEAD_DIM
D_DIL = N_HEADS_DIL * HEAD_DIM
D_MEM = N_HEADS_MEM * HEAD_DIM
D_MIX = D_MOBA + D_DIL + D_MEM
D_IN = 4 * D_MOBA + 4 * D_DIL + 2 * D_MEM
N_MEM = 256
MOBA_BLOCK = 256
MOBA_TOPK = 3
MOBA_Q_CHUNK = 32
DIL_PATTERNS = ((128, 1), (512, 4), (2048, 16))


def rms_norm(x, g):
    xf = x.astype(jnp.float32)
    y = xf * lax.rsqrt(jnp.mean(xf * xf, axis=-1, keepdims=True) + EPS)
    return (y * g.astype(jnp.float32)).astype(x.dtype)

def rope(x):
    T = x.shape[2]
    half = HEAD_DIM // 2
    inv = ROPE_THETA ** (-jnp.arange(half, dtype=jnp.float32) / half)
    ang = jnp.arange(T, dtype=jnp.float32)[:, None] * inv[None, :]
    cos, sin = jnp.cos(ang), jnp.sin(ang)
    x1 = x[..., :half].astype(jnp.float32)
    x2 = x[..., half:].astype(jnp.float32)
    out = jnp.concatenate([x1 * cos - x2 * sin, x2 * cos + x1 * sin], axis=-1)
    return out.astype(x.dtype)

def to_heads(t, n):
    B, T, _ = t.shape
    return t.reshape(B, T, n, HEAD_DIM).transpose(0, 2, 1, 3)

def from_heads(t):
    B, H, T, dh = t.shape
    return t.transpose(0, 2, 1, 3).reshape(B, T, H * dh)

def moba_attention(q, k, v):
    B, H, T, dh = q.shape
    nb = -(-T // MOBA_BLOCK)
    Tp = nb * MOBA_BLOCK
    pad = ((0, 0), (0, 0), (0, Tp - T), (0, 0))
    q, k, v = jnp.pad(q, pad), jnp.pad(k, pad), jnp.pad(v, pad)
    kb = k.reshape(B, H, nb, MOBA_BLOCK, dh)
    vb = v.reshape(B, H, nb, MOBA_BLOCK, dh)
    k_mean = jnp.mean(kb.astype(jnp.float32), axis=3)
    topk = min(MOBA_TOPK, nb - 1)
    n_chunks = Tp // MOBA_Q_CHUNK
    q_chunks = q.reshape(B, H, n_chunks, MOBA_Q_CHUNK, dh).transpose(2, 0, 1, 3, 4)
    b_ix = jnp.arange(B)[:, None, None, None]
    h_ix = jnp.arange(H)[None, :, None, None]
    scale = dh ** -0.5

    def one_chunk(args):
        ci, qc = args
        start = ci * MOBA_Q_CHUNK
        c = start // MOBA_BLOCK
        q_pos = start + jnp.arange(MOBA_Q_CHUNK)
        k_pos = c * MOBA_BLOCK + jnp.arange(MOBA_BLOCK)
        own_k = lax.dynamic_index_in_dim(kb, c, axis=2, keepdims=False)
        own_v = lax.dynamic_index_in_dim(vb, c, axis=2, keepdims=False)
        s_own = jnp.einsum('bhqd,bhkd->bhqk', qc, own_k).astype(jnp.float32) * scale
        s_own = jnp.where(k_pos[None, :] <= q_pos[:, None], s_own, -jnp.inf)
        if topk == 0:
            p = jax.nn.softmax(s_own, axis=-1).astype(vb.dtype)
            return jnp.einsum('bhqk,bhkd->bhqd', p, own_v)
        gate = jnp.einsum('bhqd,bhnd->bhqn', qc.astype(jnp.float32), k_mean)
        gate = jnp.where(jnp.arange(nb) < c, gate, -jnp.inf)
        _, idx = lax.top_k(gate, topk)
        valid = idx < c
        sel_k = kb[b_ix, h_ix, idx]
        sel_v = vb[b_ix, h_ix, idx]
        s_sel = jnp.einsum('bhqd,bhqnkd->bhqnk', qc, sel_k).astype(jnp.float32) * scale
        s_sel = jnp.where(valid[..., None], s_sel, -jnp.inf)
        s_sel = s_sel.reshape(B, H, MOBA_Q_CHUNK, topk * MOBA_BLOCK)
        p = jax.nn.softmax(jnp.concatenate([s_own, s_sel], axis=-1), axis=-1).astype(vb.dtype)
        p_own = p[..., :MOBA_BLOCK]
        p_sel = p[..., MOBA_BLOCK:].reshape(B, H, MOBA_Q_CHUNK, topk, MOBA_BLOCK)
        return (jnp.einsum('bhqk,bhkd->bhqd', p_own, own_v)
                + jnp.einsum('bhqnk,bhqnkd->bhqd', p_sel, sel_v))

    out = lax.map(one_chunk, (jnp.arange(n_chunks, dtype=jnp.int32), q_chunks))
    return out.transpose(1, 2, 0, 3, 4).reshape(B, H, Tp, dh)[:, :, :T]

def dilated_attention(q, k, v):
    B, H, T, dh = q.shape
    scale = dh ** -0.5
    outs, lses = [], []
    for window, dil in DIL_PATTERNS:
        W = window // dil
        n = -(-T // (W * dil))
        L = n * W * dil
        pad = ((0, 0), (0, 0), (0, L - T), (0, 0))

        def split(t):
            return jnp.pad(t, pad).reshape(B, H, n, W, dil, dh).transpose(0, 1, 4, 2, 3, 5)

        qs, ks, vs = split(q), split(k), split(v)
        prev = ((0, 0), (0, 0), (0, 0), (1, 0), (0, 0), (0, 0))
        k_cat = jnp.concatenate([jnp.pad(ks, prev)[:, :, :, :-1], ks], axis=4)
        v_cat = jnp.concatenate([jnp.pad(vs, prev)[:, :, :, :-1], vs], axis=4)
        s = jnp.einsum('bhrnqd,bhrnkd->bhrnqk', qs, k_cat).astype(jnp.float32) * scale
        i = jnp.arange(W)[:, None]
        j = jnp.arange(2 * W)[None, :]
        band = (j >= i) & (j <= i + W)
        first = (jnp.arange(n)[:, None, None] > 0) | (j[None] >= W)
        s = jnp.where(band[None] & first, s, -jnp.inf)
        lse = jax.nn.logsumexp(s, axis=-1)
        p = jnp.exp(s - lse[..., None]).astype(v.dtype)
        o = jnp.einsum('bhrnqk,bhrnkd->bhrnqd', p, v_cat)
        outs.append(o.transpose(0, 1, 3, 4, 2, 5).reshape(B, H, L, dh)[:, :, :T])
        lses.append(lse.transpose(0, 1, 3, 4, 2).reshape(B, H, L)[:, :, :T])
    w = jax.nn.softmax(jnp.stack(lses, axis=0), axis=0)
    o_all = jnp.stack(outs, axis=0).astype(jnp.float32)
    return jnp.einsum('pbht,pbhtd->bhtd', w, o_all).astype(q.dtype)

def memory_attention(q, k, v):
    s = jnp.einsum('bhqd,bhkd->bhqk', q, k).astype(jnp.float32) * (HEAD_DIM ** -0.5)
    p = jax.nn.softmax(s, axis=-1).astype(v.dtype)
    return jnp.einsum('bhqk,bhkd->bhqd', p, v)

def hybrid_layer(x, mem, norm_g, w_in, w_out, mem_norm_g, w_mem_kv, qk_g):
    h = rms_norm(x, norm_g)
    proj = jnp.einsum('btd,de->bte', h, w_in)
    sizes = [D_MOBA] * 4 + [D_DIL] * 4 + [D_MEM] * 2
    cuts = [int(c) for c in np.cumsum(sizes)[:-1]]
    a_q, a_k, a_v, a_g, b_q, b_k, b_v, b_g, m_q, m_g = jnp.split(proj, cuts, axis=-1)

    qa = rope(rms_norm(to_heads(a_q, N_HEADS_MOBA), qk_g[0]))
    ka = rope(rms_norm(to_heads(a_k, N_HEADS_MOBA), qk_g[1]))
    oa = from_heads(moba_attention(qa, ka, to_heads(a_v, N_HEADS_MOBA)))

    qb = rope(rms_norm(to_heads(b_q, N_HEADS_DIL), qk_g[2]))
    kb = rope(rms_norm(to_heads(b_k, N_HEADS_DIL), qk_g[3]))
    ob = from_heads(dilated_attention(qb, kb, to_heads(b_v, N_HEADS_DIL)))

    mkv = jnp.einsum('bmd,de->bme', rms_norm(mem, mem_norm_g), w_mem_kv)
    m_k, m_v = jnp.split(mkv, 2, axis=-1)
    qm = rms_norm(to_heads(m_q, N_HEADS_MEM), qk_g[4])
    km = rms_norm(to_heads(m_k, N_HEADS_MEM), qk_g[5])
    om = from_heads(memory_attention(qm, km, to_heads(m_v, N_HEADS_MEM)))

    y = jnp.concatenate([oa * jax.nn.silu(a_g), ob * jax.nn.silu(b_g), om * jax.nn.silu(m_g)], axis=-1)
    return x + jnp.einsum('bte,ed->btd', y, w_out)

def second_inputs(seed: int = 0) -> dict:
    key = jax.random.key(seed)
    ks = jax.random.split(key, 10)
    f32 = jnp.float32
    x = jax.random.normal(ks[0], (BATCH, SEQ, D_MODEL), f32)
    mem = jax.random.normal(ks[1], (BATCH, N_MEM, D_MODEL), f32)
    norm_g = 1.0 + 0.02 * jax.random.normal(ks[2], (DEPTH, D_MODEL), f32)
    w_in = jax.random.normal(ks[3], (DEPTH, D_MODEL, D_IN), f32) * D_MODEL ** -0.5
    w_out = jax.random.normal(ks[4], (DEPTH, D_MIX, D_MODEL), f32) * (D_MIX ** -0.5) / math.sqrt(2 * DEPTH)
    mem_norm_g = 1.0 + 0.02 * jax.random.normal(ks[5], (DEPTH, D_MODEL), f32)
    w_mem_kv = jax.random.normal(ks[6], (DEPTH, D_MODEL, 2 * D_MEM), f32) * D_MODEL ** -0.5
    qk_g = 1.0 + 0.02 * jax.random.normal(ks[7], (DEPTH, 6, HEAD_DIM), f32)
    return {"x": x, "mem": mem, "norm_g": norm_g, "w_in": w_in, "w_out": w_out,
            "mem_norm_g": mem_norm_g, "w_mem_kv": w_mem_kv, "qk_g": qk_g}

def second_block(x, mem, norm_g, w_in, w_out, mem_norm_g, w_mem_kv, qk_g):
    for layer in range(DEPTH):
        x = hybrid_layer(x, mem, norm_g[layer], w_in[layer], w_out[layer],
                         mem_norm_g[layer], w_mem_kv[layer], qk_g[layer])
    return x


def setup_inputs(seed=0):
    out = dict(first_inputs(seed))
    for name, value in second_inputs(seed + 1).items():
        if name != "x":
            out[name + "_2"] = value
    return out


def reference(
    x, positions, norm_g, w_in, b_gate, sg_ln_g, sg_ln_b, sg_w, sg_b, mla_cq_g, mla_ckv_g,
    mla_w_uq, mla_w_ukv, mla_q_g, mla_k_g, gla_w_gate, gla_b_gate, gla_o_g, w_branch, w_out,
    mem_2, norm_g_2, w_in_2, w_out_2, mem_norm_g_2, w_mem_kv_2, qk_g_2,
):
    x = first_block(
        x, positions, norm_g, w_in, b_gate, sg_ln_g, sg_ln_b, sg_w, sg_b, mla_cq_g, mla_ckv_g,
        mla_w_uq, mla_w_ukv, mla_q_g, mla_k_g, gla_w_gate, gla_b_gate, gla_o_g, w_branch, w_out,
    )
    return second_block(
        x, mem_2, norm_g_2, w_in_2, w_out_2, mem_norm_g_2, w_mem_kv_2, qk_g_2,
    )


_drawn_inputs = setup_inputs


def setup_inputs(seed=0):
    import zlib

    import numpy as np

    out = dict(_drawn_inputs(seed))
    spreads = {}
    factors = {'sg_ln_g': 8.0,
     'sg_ln_b': 8.0,
     'sg_b': 8.0,
     'mla_cq_g': 8.0,
     'mla_ckv_g': 8.0,
     'mla_q_g': 8.0,
     'mla_k_g': 8.0,
     'gla_b_gate': 2.834,
     'gla_o_g': 6.765,
     'mem_2': 3.135,
     'norm_g_2': 8.0,
     'mem_norm_g_2': 8.0,
     'w_mem_kv_2': 3.024,
     'qk_g_2': 8.0}
    for name, (base, spread) in spreads.items():
        noise = np.random.default_rng([zlib.crc32(name.encode()), seed]).standard_normal(out[name].shape)
        drawn = base * np.exp(spread * noise) if base else spread * noise
        out[name] = __import__('jax').numpy.asarray(drawn.astype(out[name].dtype))
    for name, factor in factors.items():
        out[name] = (out[name] * factor).astype(out[name].dtype)
    return out
```

```python
import math
from contextlib import ExitStack

import numpy as np
import concourse.bass as bass
from concourse import mybir

F32 = mybir.dt.float32
F32R = mybir.dt.float32r
I32 = mybir.dt.int32
ALU = mybir.AluOpType
ACT = mybir.ActivationFunctionType
AX_X = mybir.AxisListType.X

P = 128
T = 512
NT = T // P
D = 1024
KD = D // P
DEPTH = 2
EPS = 1e-6
NEG = -1.0e30

CHUNK = 64
BW = 512
MH, NOPE, ROPE, MV = 8, 64, 32, 64
QK = NOPE + ROPE
HALF = ROPE // 2
QR, KVR = 256, 128
GH, DK, DV, GR, TAU = 4, 64, 128, 16, 16.0
C_U, C_V, C_ZA = 0, BW, 2 * BW
C_C = 3 * BW
NC_C = QR + KVR + ROPE
C_ZB = C_C + NC_C
C_QC = C_ZB + MH * MV
C_VC = C_QC + 2 * GH * DK
C_GC = C_VC + GH * DV
C_ZC = C_GC + GR
C_GATE = C_ZC + GH * DV

HD = 64
AH, BH, EH = 6, 6, 4
NMEM = 256
WA, WB, WE = AH * HD, BH * HD, EH * HD

TWO_PI = 2.0 * math.pi
PI_1 = 6.28125
PI_2 = float((np.array([np.float32(TWO_PI - PI_1)]).view(np.uint32) & np.uint32(0xFFFFF000)).view(np.float32)[0])
PI_3 = float(np.float32(TWO_PI - PI_1 - PI_2))
ROUND = 12582912.0

RING = 4
AHEAD = RING - 1
RAW = 4
PIECE = 2


def constants():
    p = np.arange(P)[:, None]
    c = np.arange(T)[None, :]
    d = (T - P) + p - c
    diag = c - (T - P)
    out = {}
    out["k_ident"] = np.eye(P, dtype=np.float32)
    out["k_mask_chunk"] = np.where((diag >= 0) & (diag // CHUNK > p // CHUNK), NEG, 0.0).astype(np.float32)
    out["k_mask_causal"] = np.where(d < 0, NEG, 0.0).astype(np.float32)
    count = ((d >= 0) & (d <= 128)).astype(int) + ((d >= 0) & (d % 4 == 0)) + ((d >= 0) & (d % 16 == 0))
    bias = np.where(count > 0, np.log(np.maximum(count, 1)) / (HD ** -0.5), NEG)
    out["k_mask_dilated"] = bias.astype(np.float32)
    j, i = np.arange(P)[:, None], np.arange(P)[None, :]
    keep = ((j <= i) & (j // CHUNK == i // CHUNK)).astype(np.int32)
    out["k_keep"] = np.tile(keep, (1, NT)).astype(np.int32)
    out["k_carry"] = np.tile((np.arange(T) % CHUNK != 0).astype(np.float32), (P, 1))
    inv = (np.float32(1.0) / np.power(np.float32(10000.0), np.arange(HALF, dtype=np.float32) * np.float32(2.0)
                                      / np.float32(ROPE))).astype(np.float32)
    out["k_inv"] = np.tile(inv, (P, 1)).astype(np.float32)
    inv2 = np.power(np.float32(10000.0), -np.arange(HD // 2, dtype=np.float32) / np.float32(HD // 2)).astype(np.float32)
    ang = np.arange(T, dtype=np.float32)[:, None] * inv2[None, :]
    out["k_cos2"] = np.cos(ang).astype(np.float32)
    out["k_sin2"] = np.sin(ang).astype(np.float32)
    return out


class Group:

    def __init__(self, src, K, n, banks):
        self.src, self.K, self.n, self.banks = src, K, n, banks


def plan_groups(w):
    groups, index = [], {}

    def add(key, src, K, n, banks):
        index[key] = len(groups)
        groups.append(Group(src, K, n, banks))

    def cols(name, l, c0, n):
        return lambda k0, k1: w[name][l, k0 * P:k1 * P, c0:c0 + n]

    for l in range(DEPTH):
        def one(tag, c0, n, banks=4):
            add((1, l, tag), cols("w_in", l, c0, n), KD, n, banks)
        one("c", C_C, NC_C)
        one("v", C_V, BW)
        one("u", C_U, BW)
        one("za", C_ZA, BW)
        one("zb", C_ZB, MH * MV)
        for i in range(2):
            add((1, l, "uq", i), cols("mla_w_uq", l, i * 4 * QK, 4 * QK), QR // P, 4 * QK, 4)
        for i in range(2):
            add((1, l, "ukv", i), cols("mla_w_ukv", l, i * 4 * (NOPE + MV), 4 * (NOPE + MV)), 1, 4 * (NOPE + MV), 4)
        one("qkc", C_QC, 2 * GH * DK)
        one("gc", C_GC, P, 1)
        one("vc", C_VC, GH * DV)
        one("zc", C_ZC, GH * DV)
        for j in range(2):
            for i in range(3):
                one(("gate", j, i), C_GATE + i * D + j * T, T)
                def branch(k0, k1, i=i, j=j, l=l):
                    return w["w_branch"][l, i, k0 * P:k1 * P, j * T:(j + 1) * T]
                add((1, l, "branch", j, i), branch, BW // P, T, 4)
        for j in range(2):
            add((1, l, "out", j), cols("w_out", l, j * T, T), KD, T, 4)
    for l in range(DEPTH):
        def two(tag, c0, n, banks=4, name="w_in_2"):
            add((2, l, tag), cols(name, l, c0, n), KD, n, banks)
        two("mkv", 0, 2 * WE, NMEM // P, "w_mem_kv_2")
        two("aq", 0, WA)
        two("ak", WA, WA)
        two("av", 2 * WA, WA)
        two("bq", 4 * WA, WB)
        two("bk", 4 * WA + WB, WB)
        two("bv", 4 * WA + 2 * WB, WB)
        two("ag", 3 * WA, WA)
        two("m", 4 * WA + 4 * WB, 2 * WE)
        two("bg", 4 * WA + 3 * WB, WB)
        for j in range(2):
            add((2, l, "out", j), cols("w_out_2", l, j * T, T), KD, T, 4)
    return groups, index


def hybrid_kernel(nc, w, out, stack):
    groups, gindex = plan_groups(w)
    first_step, step_group = [], []
    first_piece, pieces = [], []
    for gi, g in enumerate(groups):
        first_step.append(len(step_group))
        first_piece.append(len(pieces))
        step_group += [(gi, k) for k in range(g.K)]
        pieces += [(gi, k0, min(g.K, k0 + PIECE)) for k0 in range(0, g.K, PIECE)]
    bank_use, bank_uses = {}, [0] * 4
    for gi, g in enumerate(groups):
        for b in range(g.banks):
            bank_use[gi, b] = bank_uses[b]
            bank_uses[b] += 1
    steps_marked = []
    for s, (gi, k) in enumerate(step_group):
        steps_marked.append((steps_marked[-1] if s else 0) + (k != groups[gi].K - 1))

    SBUF_0 = 16512
    KB = 1024
    top = [SBUF_0]

    def at(name, shape, dt, offset):
        return nc.alloc_sbuf_tensor_at(name, shape, dt, offset=offset)

    def place(name, shape, dt=F32):
        size = 4 * int(np.prod(shape[1:]))
        t = at(name, shape, dt, top[0])
        top[0] += (size + 31) // 32 * 32
        return t

    def area(size):
        a = top[0]
        top[0] += size
        return a

    x = place("x", [P, NT, D])
    act_hi = place("act_hi", [P, KD, T], F32R)
    act_lo = place("act_lo", [P, KD, T], F32R)
    raw = place("raw", [P, RAW, PIECE, T])
    w_hi = place("w_hi", [P, RING, T], F32R)
    w_lo = place("w_lo", [P, RING, T], F32R)
    ident = place("ident", [P, P])
    mask_chunk = place("mask_chunk", [P, T])
    mask_causal = place("mask_causal", [P, T])
    mask_dilated = place("mask_dilated", [P, T])
    inv_freq = place("inv_freq", [P, HALF])
    cos1 = place("cos1", [P, NT, HALF])
    sin1 = place("sin1", [P, NT, HALF])
    cos2 = place("cos2", [P, NT, HD // 2])
    sin2 = place("sin2", [P, NT, HD // 2])
    minus_half = place("minus_half", [P, 64])
    R_GATE, R_X, R_MEM, R_POS, R_C, R_GLA = 0, 48, 80, 96, 100, 106
    N_ROWS = 110
    vec_cols = place("vec_cols", [P, N_ROWS])
    w_gu = place("w_gu", [GR, DEPTH, GH * DK])
    gain_q = place("gain_q", [P, DEPTH, QK])
    gain_k = place("gain_k", [P, DEPTH, QK])
    gain_o = place("gain_o", [P, DEPTH, DV])
    gain_2 = place("gain_2", [P, DEPTH, 6, HD])
    sums = place("sums", [P, 64])
    mean_sq = place("mean_sq", [P, 64])
    rstd = place("rstd", [P, 64])
    stats6 = place("stats6", [P, NT, 6])
    mean_var = place("mean_var", [P, NT, 2])
    neg_max = place("neg_max", [P, 64])
    row_sum = place("row_sum", [P, 64])
    row_inv = place("row_inv", [P, 64])

    Y = area(48 * KB)
    A = area(0)
    END = 229344
    assert A + 60 * KB <= END, (A, END, (END - A) / 1024)

    vec_rows = at("vec_rows", [P, P], F32, A)
    pos_rows = at("pos_rows", [P, P], I32, A + KB)
    angle = at("angle", [P, 4, NT, HALF], F32, A + 8 * KB)
    y_hi = [at(f"y{i}_hi", [P, 4, T], F32R, Y + 16 * KB * i) for i in range(3)]
    y_lo = [at(f"y{i}_lo", [P, 4, T], F32R, Y + 16 * KB * i + 8 * KB) for i in range(3)]
    zb = at("zb", [P, NT, MH * MV], F32, Y + 16 * KB)
    v_mla = at("v_mla", [P, NT, MH, MV], F32, Y + 24 * KB)
    za = at("za", [P, 4, T], F32, Y + 32 * KB)
    vn = at("vn", [P, NT, BW], F32, Y + 40 * KB)
    vc = at("vc", [P, NT, GH * DV], F32, Y + 32 * KB)
    zc = at("zc", [P, NT, GH * DV], F32, Y + 40 * KB)
    u = at("u", [P, 4, T], F32, A)
    qk_c = at("qk_c", [P, 4, T], F32, A)
    q = at("q", [P, NT, MH, QK], F32, A + 8 * KB)
    k = at("k", [P, NT, MH, QK], F32, A + 20 * KB)
    sg_w_raw = at("sg_w_raw", [P, 4, P], F32, A + 20 * KB)
    sg_wT = at("sg_wT", [P, 4, P], F32, A + 22 * KB)
    sg_bias = at("sg_bias", [P, 4, P], F32, A + 24 * KB)
    ln_g = at("ln_g", [P, BW], F32, A + 26 * KB)
    ln_b = at("ln_b", [P, BW], F32, A + 28 * KB)
    W1 = A + 32 * KB
    g_T = at("g_T", [GR, T], F32, W1 + 20 * KB)
    yb_tok = at("yb_tok", [P, NT, MH * MV], F32, W1 + 8 * KB)
    c_tok = at("c_tok", [P, NT, NC_C], F32, W1)
    c_sq = at("c_sq", [P, NC_C], F32, W1 + 6784)
    c_hi = at("c_hi", [P, 3, T], F32R, W1 + 9 * KB)
    c_lo = at("c_lo", [P, 3, T], F32R, W1 + 15 * KB)
    sq_1 = at("sq_1", [P, MH, QK], F32, W1 + 6784)
    rope_1 = [at(f"rope_1{i}", [P, NT, MH, HALF], F32, W1 + 10 * KB + 2 * KB * i) for i in range(4)]
    x_n = [at("x_n1", [P, NT, D], F32, W1), at("x_n2", [P, NT, D], F32, Y)]
    merged = at("merged", [P, KD, T], F32, A)
    gate = at("gate", [P, 2, 4, T], F32, A + 16 * KB)
    product = at("product", [P, 2, T], F32, A + 32 * KB)
    kt_pad = at("kt_pad", [P, 2, 2, T], F32, A + 8 * KB)
    ks_tok = at("ks_tok", [P, NT, GH * DK], F32, A + 16 * KB)
    keep = at("keep", [P, NT, P], I32, A + 20 * KB)
    carry = at("carry", [P, T], F32, A + 22 * KB)
    log_a = at("log_a", [P, 2, T], F32, A + 24 * KB)
    log_t = at("log_t", [P, 2, T], F32, A + 28 * KB)
    b_cum = at("b_cum", [P, 2, T], F32, A + 32 * KB)
    e_up = at("e_up", [P, 2, T], F32, A + 36 * KB)
    e_dn = at("e_dn", [P, 2, T], F32, A + 40 * KB)
    e_st = at("e_st", [P, 2, T], F32, A + 44 * KB)
    att = at("att", [P, GH, NT, P], F32, A + 24 * KB)
    state = at("state", [P, T // CHUNK - 1, 2, 2 * DV], F32, A + 32 * KB)
    o_tok = at("o_tok", [P, NT, GH * DV], F32, A + 46 * KB)
    o_sq = at("o_sq", [P, GH * DV], F32, A + 54 * KB)
    decay = at("decay", [P, 2, T // CHUNK], F32, A + 56 * KB)
    kinds = {n: at(n, [P, NT, AH, HD], F32, Y + 6 * KB * i)
             for i, n in enumerate(["aq", "ak", "av", "bq", "bk", "bv", "ag", "bg"])}
    m_flat = at("m_flat", [P, NT, 2 * WE], F32, A)
    mkv_flat = at("mkv_flat", [P, NMEM // P, 2 * WE], F32, A + 8 * KB)
    m_tok = m_flat[:, :, :].rearrange("p t (s h d) -> p t s h d", s=2, h=EH)
    mkv = mkv_flat[:, :, :].rearrange("p t (s h d) -> p t s h d", s=2, h=EH)
    W2 = A + 12 * KB
    mem_x = at("mem_x", [P, NMEM // P, D], F32, W2)
    mem_n = at("mem_n", [P, NMEM // P, D], F32, W2 + 8 * KB)
    rope_2 = [at(f"rope_2{i}", [P, NT, AH, HD // 2], F32, A + 32 * KB + 3 * KB * i) for i in range(4)]
    sq_2 = at("sq_2", [P, AH, HD], F32, A + 44 * KB)
    mem_hi = at("mem_hi", [P, KD, NMEM], F32R, A + 44 * KB)
    mem_lo = at("mem_lo", [P, KD, NMEM], F32R, A + 52 * KB)
    qT, kT, masked, probs, probsT = [
        [at(f"{n}{i + 1}", [P, 2, T], F32, base + 4 * KB * j) for i, base in enumerate([W1, W2])]
        for j, n in enumerate(["qT", "kT", "masked", "probs", "probsT"])]

    def spread(ap):
        return ap.partition_broadcast(P)

    const_loads = [
        (ident[:, :], w["k_ident"]), (mask_chunk[:, :], w["k_mask_chunk"]),
        (mask_causal[:, :], w["k_mask_causal"]), (mask_dilated[:, :], w["k_mask_dilated"]),
        (inv_freq[:, :], w["k_inv"]), (cos2[:, :, :], w["k_cos2"].rearrange("(t p) f -> p t f", p=P)),
        (sin2[:, :, :], w["k_sin2"].rearrange("(t p) f -> p t f", p=P)),
        (pos_rows[R_POS:R_POS + NT, :], w["positions"].rearrange("a (t p) -> (a t) p", p=P)),
    ]

    def rows_at(r, ap):
        n = ap.shape[0] // P
        return vec_rows[r:r + n, :], ap.rearrange("(k p) -> k p", p=P)

    for l in range(DEPTH):
        const_loads += [
            rows_at(R_GATE + 3 * KD * l, w["b_gate"][l]),
            rows_at(R_X + KD * l, w["norm_g"][l]),
            rows_at(R_X + KD * (DEPTH + l), w["norm_g_2"][l]),
            rows_at(R_MEM + KD * l, w["mem_norm_g_2"][l]),
            rows_at(R_C + 3 * l, w["mla_cq_g"][l]),
            rows_at(R_C + 3 * l + 2, w["mla_ckv_g"][l]),
            rows_at(R_GLA + 2 * l, w["gla_b_gate"][l]),
            (w_gu[:, l, :], w["gla_w_gate"][l]),
            (gain_q[:, l, :], spread(w["mla_q_g"][l])), (gain_k[:, l, :], spread(w["mla_k_g"][l])),
            (gain_o[:, l, :], spread(w["gla_o_g"][l])), (gain_2[:, l, :, :], spread(w["qk_g_2"][l])),
        ]

    def vec_col(r, n=1):
        return vec_cols[:, r:r + n]

    N_CONST = len(const_loads)

    gemm_bank = [stack.enter_context(nc.psum_tensor(f"gemm_bank{b}", [P, T], F32)) for b in range(4)]
    aux_bank = [stack.enter_context(nc.psum_tensor(f"aux_bank{b}", [P, T], F32)) for b in range(4)]

    def sem(name):
        return stack.enter_context(nc.semaphore(name))

    consts_loaded = sem("consts_loaded")
    x_loaded = sem("x_loaded")
    mem_loaded = sem("mem_loaded")
    sg_loaded = sem("sg_loaded")
    gla_loaded = sem("gla_loaded")
    raw_loaded = [sem(f"raw_loaded{i}") for i in range(RAW)]
    w_hi_ready = sem("w_hi_ready")
    w_lo_ready = sem("w_lo_ready")
    w_used = sem("w_used")
    gemm_full = [sem(f"gemm_full{b}") for b in range(4)]
    gemm_read = [sem(f"gemm_read{b}") for b in range(4)]
    aux_full = [sem(f"aux_full{b}") for b in range(4)]
    aux_read = [sem(f"aux_read{b}") for b in range(4)]
    scalar_done = sem("scalar_done")
    vector_done = sem("vector_done")
    pool_done = sem("pool_done")
    squares_ready = sem("squares_ready")
    sums_ready = sem("sums_ready")
    rstd_ready = sem("rstd_ready")
    rows_scaled = sem("rows_scaled")
    feat_hi_ready = sem("feat_hi_ready")
    positions_ready = sem("positions_ready")
    rope_ready = sem("rope_ready")
    sines_ready = sem("sines_ready")
    c_scaled = sem("c_scaled")
    vn_ready = sem("vn_ready")
    ya_ready = sem("ya_ready")
    ya_hi_ready = sem("ya_hi_ready")
    ya_lo_ready = sem("ya_lo_ready")
    heads_ready = sem("heads_ready")
    rows_gated = sem("rows_gated")
    probs_ready = sem("probs_ready")
    silu_ready = sem("silu_ready")
    gla_gate = sem("gla_gate")
    gla_exp = sem("gla_exp")
    gla_qk = sem("gla_qk")
    pads_zeroed = sem("pads_zeroed")
    gate_ready = sem("gate_ready")
    merged_ready = sem("merged_ready")
    merged_hi_ready = sem("merged_hi_ready")
    merged_lo_ready = sem("merged_lo_ready")
    out_stored = sem("out_stored")

    UNITS_1, UNITS_2 = MH * NT, (AH + BH + EH) * NT

    group_key = {gi: key for key, gi in gindex.items()}

    def gi_of(*key):
        return gindex[key]

    def wait_gemm_full(eng, gi, b):
        eng.wait_ge(gemm_full[b], bank_use[gi, b] + 1)

    def wait_gemm_read(eng, gi, b=None):
        for i in (range(groups[gi].banks) if b is None else [b]):
            eng.wait_ge(gemm_read[i], bank_use[gi, i] + 1)

    def wait_group_done(eng, gi):
        wait_gemm_full(eng, gi, groups[gi].banks - 1)

    def wait_step_used(eng, s):
        gi, kk = step_group[s]
        if kk == groups[gi].K - 1:
            wait_group_done(eng, gi)
        else:
            eng.wait_ge(w_used, steps_marked[s])

    aux_place = {}
    aux_count = [0]

    def aux_open(key):
        n = aux_count[0]
        aux_count[0] += 1
        b, use = n % 4, n // 4
        assert key not in aux_place, key
        aux_place[key] = (b, use)
        if use:
            nc.tensor.wait_ge(aux_read[b], use)
        return aux_bank[b]

    def aux_wait_full(eng, key):
        b, use = aux_place[key]
        eng.wait_ge(aux_full[b], use + 1)
        return aux_bank[b]

    def aux_wait_read(eng, key):
        b, use = aux_place[key]
        eng.wait_ge(aux_read[b], use + 1)

    def full_of(key):
        return aux_full[aux_place[key][0]]

    def read_of(key):
        return aux_read[aux_place[key][0]]

    def flat_2(name):
        return m_flat if name == "m" else kinds[name][:, :, :, :].rearrange("p t h d -> p t (h d)")

    def y2_key(l, kk):
        return [((2, l, "yaq", kk)), (2, l, "ybq", kk - 3), (2, l, "ym", kk - 6)][min(kk // 3, 2)]

    block = stack.enter_context(nc.Block())

    BESIDE = {("mla", l): [(1, l, g) for g in ("qkc", "gc", "vc", "zc")] for l in range(DEPTH)}
    BESIDE |= {("moba", l): [(2, l, g) for g in ("bq", "bk", "bv")] for l in range(DEPTH)}
    BESIDE |= {("dilated", l): [(2, l, g) for g in ("ag", "m", "bg")] for l in range(DEPTH)}
    BESIDE |= {("memory", l): [] for l in range(DEPTH)}

    def beside(name, l, n_units):
        keys = [gindex[g] for g in BESIDE[name, l]]
        steps = [first_step[gi] + kk for gi in keys for kk in range(groups[gi].K)]
        out = []
        for n in range(n_units):
            part = steps[n * len(steps) // n_units:(n + 1) * len(steps) // n_units]
            ended = [step_group[s][0] for s in part if step_group[s][1] == groups[step_group[s][0]].K - 1]
            out.append((part, ended))
        return out

    class Attention:

        def __init__(self, name, l, heads, d, q_of, k_of, v_of, n_keys, mask, out_of, first_unit, where):
            self.name, self.l, self.heads, self.d = name, l, heads, d
            self.q_of, self.k_of, self.v_of, self.out_of = q_of, k_of, v_of, out_of
            self.n_keys, self.mask, self.first_unit, self.where = n_keys, mask, first_unit, where
            self.units = [(h, i) for h in range(heads) for i in range(NT)]
            self.k_tiles = max(n_keys(i) for i in range(NT))
            self.scale = d ** -0.5

    def attention_1(l):
        return Attention("mla", l, MH, QK,
                         lambda h, t: q[:, t, h, :], lambda h, t: k[:, t, h, :],
                         lambda h, t: v_mla[:, t, h, :], lambda i: i + 1,
                         lambda i: mask_chunk[:, T - (i + 1) * P:T],
                         lambda h, t: q[:, t, h, 0:MV], l * UNITS_1, 0)

    def attention_2(l, name):
        base = DEPTH * UNITS_1 + l * UNITS_2
        if name == "memory":
            return Attention(name, l, EH, HD,
                             lambda h, t: m_tok[:, t, 0, h, :], lambda h, t: mkv[:, t, 0, h, :],
                             lambda h, t: mkv[:, t, 1, h, :], lambda i: NMEM // P,
                             lambda i: mask_chunk[:, 0:NMEM],
                             lambda h, t: m_tok[:, t, 0, h, :], base + (AH + BH) * NT, 1)
        a = "a" if name == "moba" else "b"
        mask = mask_causal if name == "moba" else mask_dilated
        return Attention(name, l, AH, HD,
                         lambda h, t: kinds[a + "q"][:, t, h, :], lambda h, t: kinds[a + "k"][:, t, h, :],
                         lambda h, t: kinds[a + "v"][:, t, h, :], lambda i: i + 1,
                         lambda i: mask[:, T - (i + 1) * P:T],
                         lambda h, t: kinds[a + "q"][:, t, h, :],
                         base + (0 if name == "moba" else AH * NT), 1)

    @block.tensor
    def _(pe):
        def transposes(key, source, n_k, n_t, rows=P):
            for kk in range(n_k):
                bank = aux_open((*key, kk))
                for t in range(n_t):
                    last = pe.transpose(bank[0:rows, t * P:(t + 1) * P], source(t, kk), ident[:, :])
                last.then_inc(full_of((*key, kk)), 1)

        def step(s, mode, hi, lo, ready=None):
            gi, kk = step_group[s]
            g = groups[gi]
            slot = s % RING
            if ready:
                ready(kk)
            pe.wait_ge(w_lo_ready, s + 1)
            for b in range(g.banks):
                if kk == 0 and bank_use[gi, b]:
                    pe.wait_ge(gemm_read[b], bank_use[gi, b])
                begin, end = kk == 0, kk == g.K - 1
                if mode == "features":
                    m = min(P, g.n)
                    cols = slice(b * P, b * P + m)
                    o = gemm_bank[b][0:m, 0:T]
                    passes = [(w_hi[:, slot, cols], hi[:, kk, :]), (w_hi[:, slot, cols], lo[:, kk, :]),
                              (w_lo[:, slot, cols], hi[:, kk, :])]
                else:
                    o = gemm_bank[b][:, 0:g.n]
                    tok = slice(b * P, (b + 1) * P)
                    passes = [(hi[:, kk, tok], w_hi[:, slot, 0:g.n]), (hi[:, kk, tok], w_lo[:, slot, 0:g.n]),
                              (lo[:, kk, tok], w_hi[:, slot, 0:g.n])]
                for n, (a, c) in enumerate(passes):
                    last = pe.matmul(o, a, c, start=begin and n == 0, stop=end and n == 2)
                if end:
                    last.then_inc(gemm_full[b], 1)
                elif b == g.banks - 1:
                    last.then_inc(w_used, 1)

        def gemm(gi, mode, hi=act_hi, lo=act_lo, ready=None):
            for kk in range(groups[gi].K):
                step(first_step[gi] + kk, mode, hi, lo, ready)

        def normed(key, n_t, count):
            pe.wait_ge(rows_scaled, count)
            source = x_n[key[0] - 1] if key[2] == "x" else mem_n
            transposes(key, lambda t, kk: source[:, t, kk * P:(kk + 1) * P], KD, n_t)

        def part_ready(key):
            return lambda kk: aux_wait_read(pe, (*key, kk))

        def attention(a, mode_of):
            side = beside(a.name, a.l, len(a.units))
            rows = a.d

            def turn(h):
                for what, of, n in (("q", a.q_of, NT), ("k", a.k_of, a.k_tiles)):
                    transposes((a.name, a.l, what, h), lambda t, kk: of(h, t), 1, n, rows)

            def scores(n):
                h, i = a.units[n]
                if i == 0:
                    aux_wait_read(pe, (a.name, a.l, "q", h, 0))
                    aux_wait_read(pe, (a.name, a.l, "k", h, 0))
                key = (a.name, a.l, "S", n)
                bank = aux_open(key)
                pe.matmul(bank[:, 0:a.n_keys(i) * P], qT[a.where][0:rows, h % 2, i * P:(i + 1) * P],
                          kT[a.where][0:rows, h % 2, 0:a.n_keys(i) * P],
                          start=True, stop=True).then_inc(full_of(key), 1)

            def turn_probs(n):
                h, i = a.units[n]
                pe.wait_ge(probs_ready, a.first_unit + n + 1)
                key = (a.name, a.l, "T", n)
                bank = aux_open(key)
                for j in range(a.n_keys(i)):
                    last = pe.transpose(bank[:, j * P:(j + 1) * P], probs[a.where][:, n % 2, j * P:(j + 1) * P],
                                        ident[:, :])
                last.then_inc(full_of(key), 1)

            def values(n):
                h, i = a.units[n]
                aux_wait_read(pe, (a.name, a.l, "T", n))
                key = (a.name, a.l, "O", n)
                bank = aux_open(key)
                for j in range(a.n_keys(i)):
                    last = pe.matmul(bank[:, 0:HD], probsT[a.where][:, n % 2, j * P:(j + 1) * P], a.v_of(h, j),
                                     start=(j == 0), stop=(j == a.n_keys(i) - 1))
                last.then_inc(full_of(key), 1)

            turn(0)
            scores(0)
            for n, (h, i) in enumerate(a.units):
                if i == 1 and h + 1 < a.heads:
                    turn(h + 1)
                if n + 1 < len(a.units):
                    scores(n + 1)
                if n:
                    values(n - 1)
                for s in side[n][0]:
                    step(s, mode_of[group_key[step_group[s][0]]], act_hi, act_lo)
                turn_probs(n)
            values(len(a.units) - 1)

        def block_1(l):
            normed((1, l, "x"), NT, l * NT + NT)
            ready = part_ready((1, l, "x"))
            gemm(gi_of(1, l, "c"), "tokens", ready=ready)
            gemm(gi_of(1, l, "v"), "tokens")
            gemm(gi_of(1, l, "u"), "features")
            pe.wait_ge(c_scaled, l + 1)
            transposes((1, l, "c"), lambda t, kk: c_tok[:, t, kk * P:(kk + 1) * P], 3, NT)
            pe.wait_ge(sg_loaded, 64 * (l + 1))
            transposes((1, l, "sgw"), lambda t, kk: sg_w_raw[:, t, :], 1, 4)
            gemm(gi_of(1, l, "za"), "features")
            gemm(gi_of(1, l, "zb"), "tokens")
            pe.wait_ge(vn_ready, l + 1)
            aux_wait_read(pe, (1, l, "sgw", 0))
            for g in range(4):
                key = (1, l, "sv", g)
                bank = aux_open(key)
                for n in range(NT):
                    last = pe.matmul(bank[:, n * P:(n + 1) * P], vn[:, n, g * P:(g + 1) * P], sg_wT[:, g, :],
                                     start=True, stop=True)
                last.then_inc(full_of(key), 1)
            for i in range(2):
                gemm(gi_of(1, l, "uq", i), "tokens", c_hi, c_lo, part_ready((1, l, "c")))
            for i in range(2):
                gemm(gi_of(1, l, "ukv", i), "tokens", c_hi[:, 2:3, :], c_lo[:, 2:3, :],
                     lambda kk: aux_wait_read(pe, (1, l, "c", 2)))
            pe.wait_ge(heads_ready, l + 1)
            attention(attention_1(l), {(1, l, "qkc"): "features", (1, l, "gc"): "features",
                                       (1, l, "vc"): "tokens", (1, l, "zc"): "tokens"})
            pe.wait_ge(rows_gated, NT * (2 * l + 1))
            transposes((1, l, "yb"), lambda t, kk: yb_tok[:, t, kk * P:(kk + 1) * P], 4, NT)
            gla(l)
            pe.wait_ge(rows_gated, NT * (2 * l + 2))
            transposes((1, l, "yc"), lambda t, kk: o_tok[:, t, kk * P:(kk + 1) * P], 4, NT)
            for j in range(2):
                for i in range(3):
                    gemm(gi_of(1, l, ("gate", j, i)), "features")
                    if i == 0:
                        r = lambda kk: pe.wait_ge(ya_lo_ready, 4 * (l + 1))
                    else:
                        r = part_ready((1, l, "yb" if i == 1 else "yc"))
                    gemm(gi_of(1, l, "branch", j, i), "features", y_hi[i], y_lo[i], r)
            for j in range(2):
                gemm(gi_of(1, l, "out", j), "tokens",
                     ready=lambda kk: pe.wait_ge(merged_lo_ready, KD * l + kk + 1))

        def gla(l):
            wait_gemm_read(pe, gi_of(1, l, "gc"))
            for m in range(2):
                key = (1, l, "gl", m)
                bank = aux_open(key)
                pe.matmul(bank[:, :], w_gu[:, l, m * P:(m + 1) * P], g_T[:, :],
                          start=True, stop=True).then_inc(full_of(key), 1)
            pe.wait_ge(gla_qk, 2 * l + 2)
            transposes((1, l, "ks"), lambda t, kk: qk_c[:, 2 + kk, t * P:(t + 1) * P], 2, NT)
            wait_gemm_read(pe, gi_of(1, l, "vc"))
            for h in range(GH):
                key = (1, l, "att", h)
                bank = aux_open(key)
                for t in range(NT):
                    last = pe.matmul(bank[:, t * P:(t + 1) * P], kt_pad[:, h // 2, h % 2, t * P:(t + 1) * P],
                                     qk_c[:, h // 2, t * P:(t + 1) * P], start=True, stop=True)
                last.then_inc(full_of(key), 1)
            for m in range(2):
                aux_wait_read(pe, (1, l, "ks", m))
            for n in range(T // CHUNK - 1):
                key = (1, l, "U", n)
                bank = aux_open(key)
                half = slice(CHUNK * (n % 2), CHUNK * (n % 2) + CHUNK)
                for m in range(2):
                    last = pe.matmul(bank[:, m * 2 * DV:(m + 1) * 2 * DV], ks_tok[half, n // 2, m * P:(m + 1) * P],
                                     vc[half, n // 2, m * 2 * DV:(m + 1) * 2 * DV], start=True, stop=True)
                last.then_inc(full_of(key), 1)
            for t in range(NT):
                key = (1, l, "o", t)
                bank = aux_open(key)
                if t == 0:
                    for h in range(GH):
                        aux_wait_read(pe, (1, l, "att", h))
                for h in range(GH):
                    pe.matmul(bank[:, h * DV:(h + 1) * DV], att[:, h, t, :], vc[:, t, h * DV:(h + 1) * DV],
                              start=(h == 0), stop=False, skip_group_check=True)
                for par in range(2):
                    n = 2 * t + par
                    if n == 0:
                        continue
                    aux_wait_read(pe, (1, l, "U", n - 1))
                    for m in range(2):
                        last = pe.matmul(bank[par * CHUNK:(par + 1) * CHUNK, m * 2 * DV:(m + 1) * 2 * DV],
                                         qk_c[:, m, n * CHUNK:(n + 1) * CHUNK], state[:, n - 1, m, :],
                                         start=False, stop=(par == 1 and m == 1), skip_group_check=True)
                last.then_inc(full_of(key), 1)

        def block_2(l):
            normed((2, l, "mem"), NMEM // P, NT * DEPTH + (NT + NMEM // P) * l + NMEM // P)
            gemm(gi_of(2, l, "mkv"), "tokens", mem_hi, mem_lo, part_ready((2, l, "mem")))
            normed((2, l, "x"), NT, NT * DEPTH + (NT + NMEM // P) * (l + 1))
            gemm(gi_of(2, l, "aq"), "tokens", ready=part_ready((2, l, "x")))
            gemm(gi_of(2, l, "ak"), "tokens")
            gemm(gi_of(2, l, "av"), "tokens")
            modes = {(2, l, g): "tokens" for g in ("bq", "bk", "bv", "ag", "m", "bg")}
            wait_gemm_read(pe, gi_of(2, l, "av"))
            pe.wait_ge(heads_ready, DEPTH + 3 * l + 1)
            attention(attention_2(l, "moba"), modes)
            wait_gemm_read(pe, gi_of(2, l, "bv"))
            pe.wait_ge(heads_ready, DEPTH + 3 * l + 2)
            attention(attention_2(l, "dilated"), modes)
            wait_gemm_read(pe, gi_of(2, l, "mkv"))
            pe.wait_ge(heads_ready, DEPTH + 3 * l + 3)
            attention(attention_2(l, "memory"), modes)
            for n, (name, tiles) in enumerate((("aq", 3), ("bq", 3), ("m", 2))):
                pe.wait_ge(rows_gated, 2 * NT * DEPTH + NT * (3 * l + n + 1))
                flat = flat_2(name)
                transposes((2, l, "y" + name), lambda t, kk: flat[:, t, kk * P:(kk + 1) * P], tiles, NT)
            for j in range(2):
                gemm(gi_of(2, l, "out", j), "tokens", ready=lambda kk: aux_wait_read(pe, y2_key(l, kk)))

        pe.wait_ge(consts_loaded, 16 * N_CONST)
        pe.wait_ge(positions_ready, 1)
        bank = aux_open("vec")
        pe.transpose(bank[:, 0:N_ROWS], vec_rows[0:N_ROWS, :], ident[0:N_ROWS, 0:N_ROWS]).then_inc(full_of("vec"), 1)
        for l in range(DEPTH):
            block_1(l)
        for l in range(DEPTH):
            block_2(l)



    class Splitter:

        def __init__(self, do):
            self.at, self.do = 0, do

        def through(self, gi):
            self.to(first_step[gi] + groups[gi].K + AHEAD)

        def to(self, s):
            while self.at < min(s, len(step_group)):
                self.do(self.at)
                self.at += 1

    def last_step_beside(side, n, l, name):
        done = [s for part, _ in side[:n + 1] for s in part]
        return done[-1] + 1 if done else None

    @block.scalar
    def _(act):
        marks = [0]

        def mark(ins):
            ins.then_inc(scalar_done, 1)
            marks[0] += 1

        def settle():
            act.wait_ge(scalar_done, marks[0])

        def round_weights(s):
            gi, kk = step_group[s]
            p = first_piece[gi] + kk // PIECE
            n = groups[gi].n
            act.wait_ge(raw_loaded[p % RAW], 16 * (p // RAW + 1))
            if s >= RING:
                wait_step_used(act, s - RING)
            act.activation(w_hi[:, s % RING, 0:n], raw[:, p % RAW, kk % PIECE, 0:n], ACT.Copy)\
               .then_inc(w_hi_ready, 1)

        split = Splitter(round_weights)

        def squares(source, n_t, which):
            for t in range(n_t):
                act.activation(x_n[which][:, t, :], source[:, t, :], ACT.Square, scale=D ** -0.5,
                               accum_out=sums[:, t:t + 1]).then_inc(squares_ready, 1)

        def features(key, n_k, n_cols, hi, gain=None, k0=0):
            for kk in range(n_k):
                bank = aux_wait_full(act, (*key, kk))
                scale = 1.0 if gain is None else gain[:, kk:kk + 1]
                act.activation(hi[:, k0 + kk, :], bank[:, 0:n_cols], ACT.Copy, scale=scale)\
                   .then_inc(feat_hi_ready, 1)

        def evict(gi, func, dst):
            split.through(gi)
            for b in range(groups[gi].banks):
                wait_gemm_full(act, gi, b)
                act.activation(dst(b), gemm_bank[b][:, 0:groups[gi].n], func).then_inc(gemm_read[b], 1)

        def attention(a):
            side = beside(a.name, a.l, len(a.units))

            def exponentials(n):
                h, i = a.units[n]
                g = a.first_unit + n
                c = g % 64
                keys = a.n_keys(i) * P
                aux_wait_read(act, (a.name, a.l, "S", n))
                if n >= 2:
                    aux_wait_full(act, (a.name, a.l, "T", n - 2))
                act.activation(probs[a.where][:, n % 2, 0:keys], masked[a.where][:, n % 2, 0:keys], ACT.Exp,
                               bias=neg_max[:, c:c + 1], scale=-1.0, accum_out=row_sum[:, c:c + 1])\
                   .then_inc(probs_ready, 1)

            def turned(n):
                h, i = a.units[n]
                keys = a.n_keys(i) * P
                bank = aux_wait_full(act, (a.name, a.l, "T", n))
                if n >= 2:
                    aux_wait_full(act, (a.name, a.l, "O", n - 2))
                act.activation(probsT[a.where][:, n % 2, 0:keys], bank[:, 0:keys], ACT.Copy)\
                   .then_inc(read_of((a.name, a.l, "T", n)), 1)

            exponentials(0)
            for n in range(len(a.units)):
                if n + 1 < len(a.units):
                    exponentials(n + 1)
                to = last_step_beside(side, n, a.l, a.name)
                if to is not None:
                    split.to(to + AHEAD)
                turned(n)

        def block_1(l):
            if l:
                for j in range(2):
                    wait_gemm_read(act, gi_of(1, l - 1, "out", j))
            else:
                act.wait_ge(x_loaded, 16)
            squares(x, NT, 0)
            act.dma_start(sg_w_raw[:, :, :], w["sg_w"][l].rearrange("g i j -> i g j")).then_inc(sg_loaded, 16)
            act.dma_start(sg_bias[:, :, :], spread(w["sg_b"][l])).then_inc(sg_loaded, 16)
            act.dma_start(ln_g[:, :], spread(w["sg_ln_g"][l])).then_inc(sg_loaded, 16)
            act.dma_start(ln_b[:, :], spread(w["sg_ln_b"][l])).then_inc(sg_loaded, 16)
            if l == 0:
                split.to(RING)
                aux_wait_read(act, "vec")
            else:
                wait_group_done(act, gi_of(1, l - 1, "out", 1))
            features((1, l, "x"), KD, T, act_hi, vec_col(R_X + KD * l, KD))
            if l == 0:
                act.wait_ge(rope_ready, 1)
                act.activation(sin1[:, :, :], angle[:, 0, :, :], ACT.Sin).then_inc(sines_ready, 1)
                act.activation(cos1[:, :, :], angle[:, 1, :, :], ACT.Sin).then_inc(sines_ready, 1)
            evict(gi_of(1, l, "c"), ACT.Copy, lambda b: c_tok[:, b, :])
            evict(gi_of(1, l, "v"), ACT.Gelu_apprx_tanh, lambda b: vn[:, b, :])
            evict(gi_of(1, l, "u"), ACT.Gelu_apprx_tanh, lambda b: u[:, b, :])
            features((1, l, "c"), 3, T, c_hi, vec_col(R_C + 3 * l, 3))
            evict(gi_of(1, l, "za"), ACT.Silu, lambda b: za[:, b, :])
            evict(gi_of(1, l, "zb"), ACT.Silu, lambda b: zb[:, b, :])
            for g in range(4):
                act.wait_ge(ya_ready, 4 * l + g + 1)
                act.activation(y_hi[0][:, g, :], u[:, g, :], ACT.Copy).then_inc(ya_hi_ready, 1)
            for i in range(2):
                evict(gi_of(1, l, "uq", i), ACT.Copy, lambda b: q[:, b, 4 * i:4 * i + 4, :])
            for i in range(2):
                split.through(gi_of(1, l, "ukv", i))
            attention(attention_1(l))
            aux_wait_full(act, ("mla", l, "k", MH - 1, 0))
            act.dma_start(keep[:, :, :], w["k_keep"].rearrange("p (t i) -> p t i", t=NT)).then_inc(gla_loaded, 16)
            act.dma_start(carry[:, :], w["k_carry"]).then_inc(gla_loaded, 16)
            features((1, l, "yb"), 4, T, y_hi[1])
            act.wait_ge(gla_gate, 3 * l + 1)
            act.activation(log_t[:, :, :], log_t[:, :, :], ACT.Exp).then_inc(scalar_done, 1)
            marks[0] += 1
            settle()
            act.activation(log_t[:, :, :], log_t[:, :, :], ACT.Ln, bias=1.0).then_inc(gla_exp, 1)
            act.wait_ge(gla_gate, 3 * l + 2)
            act.activation(e_up[:, :, :], b_cum[:, :, :], ACT.Exp, scale=1.0 / TAU).then_inc(gla_exp, 1)
            act.activation(e_dn[:, :, :], b_cum[:, :, :], ACT.Exp, scale=-1.0 / TAU).then_inc(gla_exp, 1)
            act.wait_ge(gla_gate, 3 * l + 3)
            act.activation(e_st[:, :, :], e_st[:, :, :], ACT.Exp, scale=1.0 / TAU).then_inc(gla_exp, 1)
            wait_gemm_read(act, gi_of(1, l, "zc"))
            for t in range(NT):
                act.activation(zc[:, t, :], zc[:, t, :], ACT.Silu).then_inc(silu_ready, 1)
            for t in range(NT):
                bank = aux_wait_full(act, (1, l, "o", t))
                act.activation(o_tok[:, t, :], bank[:, :], ACT.Copy).then_inc(read_of((1, l, "o", t)), 1)
            features((1, l, "yc"), 4, T, y_hi[2])
            for j in range(2):
                for i in range(3):
                    n = 3 * j + i
                    gi = gi_of(1, l, ("gate", j, i))
                    split.through(gi)
                    for m in range(4):
                        wait_gemm_full(act, gi, m)
                        if n >= 2:
                            wait_gemm_read(act, gi_of(1, l, "branch", (n - 2) // 3, (n - 2) % 3), m)
                        c = i * KD + j * 4 + m
                        act.activation(gate[:, n % 2, m, :], gemm_bank[m][:, :], ACT.Sigmoid,
                                       bias=vec_col(R_GATE + 3 * KD * l + c)).then_inc(gemm_read[m], 1)
                    split.through(gi_of(1, l, "branch", j, i))
            wait_group_done(act, gi_of(1, l, ("gate", 1, 2)))
            for kk in range(KD):
                act.wait_ge(merged_ready, KD * l + kk + 1)
                act.activation(act_hi[:, kk, :], merged[:, kk, :], ACT.Copy).then_inc(merged_hi_ready, 1)
            for j in range(2):
                split.through(gi_of(1, l, "out", j))

        def block_2(l):
            prev = (1, DEPTH - 1) if l == 0 else (2, l - 1)
            for j in range(2):
                wait_gemm_read(act, gi_of(*prev, "out", j))
            act.dma_start(mem_x[:, :, :], w["mem_2"][0].rearrange("(t p) d -> p t d", p=P)).then_inc(mem_loaded, 16)
            squares(x, NT, 1)
            act.wait_ge(mem_loaded, 16 * (l + 1))
            for t in range(NMEM // P):
                act.activation(mem_n[:, t, :], mem_x[:, t, :], ACT.Square, scale=D ** -0.5,
                               accum_out=sums[:, NT + t:NT + t + 1]).then_inc(squares_ready, 1)
            features((2, l, "mem"), KD, NMEM, mem_hi, vec_col(R_MEM + KD * l, KD))
            evict(gi_of(2, l, "mkv"), ACT.Copy, lambda b: mkv_flat[:, b, :])
            features((2, l, "x"), KD, T, act_hi, vec_col(R_X + KD * (DEPTH + l), KD))
            for name in ("aq", "ak", "av"):
                evict(gi_of(2, l, name), ACT.Copy, lambda b: flat_2(name)[:, b, :])
            for name in ("moba", "dilated", "memory"):
                attention(attention_2(l, name))
            for n, (name, c0) in enumerate((("ag", 0), ("bg", 0), ("m", WE))):
                wait_gemm_read(act, gi_of(2, l, name))
                f = flat_2(name)
                n_c = 2 * WE if name == "m" else WA
                act.activation(f[:, :, c0:n_c], f[:, :, c0:n_c], ACT.Silu).then_inc(silu_ready, 1)
            wait_group_done(act, gi_of(2, l, "bg"))
            for name, tiles, k0 in (("aq", 3, 0), ("bq", 3, 3), ("m", 2, 6)):
                features((2, l, "y" + name), tiles, T, act_hi, None, k0)
            for j in range(2):
                split.through(gi_of(2, l, "out", j))

        for l in range(DEPTH):
            block_1(l)
        for l in range(DEPTH):
            block_2(l)

    @block.vector
    def _(dve):
        marks = [0]
        hi_count = [0]

        def mark(ins):
            ins.then_inc(vector_done, 1)
            marks[0] += 1

        def settle():
            dve.wait_ge(vector_done, marks[0])

        def residue(s):
            gi, kk = step_group[s]
            p = first_piece[gi] + kk // PIECE
            n = groups[gi].n
            dve.wait_ge(w_hi_ready, s + 1)
            dve.tensor_tensor(w_lo[:, s % RING, 0:n], raw[:, p % RAW, kk % PIECE, 0:n],
                              w_hi[:, s % RING, 0:n].bitcast(F32), ALU.subtract).then_inc(w_lo_ready, 1)

        split = Splitter(residue)
        norms = [0]
        scaled = [0]

        def scale_rows(source, dst, n_t, job, s0=0):
            dve.wait_ge(rstd_ready, job)
            for t in range(n_t):
                dve.tensor_scalar(dst[:, t, :], source[:, t, :], rstd[:, s0 + t:s0 + t + 1], None, ALU.mult)\
                   .then_inc(rows_scaled, 1)

        def features(key, n_k, n_cols, hi, lo, gain=None, k0=0):
            for kk in range(n_k):
                hi_count[0] += 1
                dve.wait_ge(feat_hi_ready, hi_count[0])
                bank = aux_bank[aux_place[(*key, kk)][0]]
                h = hi[:, k0 + kk, :].bitcast(F32)
                if gain is None:
                    ins = dve.tensor_tensor(lo[:, k0 + kk, :], bank[:, 0:n_cols], h, ALU.subtract)
                else:
                    ins = dve.scalar_tensor_tensor(out=lo[:, k0 + kk, :], in0=bank[:, 0:n_cols],
                                                   scalar=gain[:, kk:kk + 1], in1=h,
                                                   op0=ALU.mult, op1=ALU.subtract)
                ins.then_inc(read_of((*key, kk)), 1)

        def evict(gi, dst):
            split.through(gi)
            evict_now(gi, dst)

        def evict_now(gi, dst, rows=P):
            for b in range(groups[gi].banks):
                wait_gemm_full(dve, gi, b)
                dve.tensor_copy(dst(b), gemm_bank[b][0:rows, 0:groups[gi].n]).then_inc(gemm_read[b], 1)

        def head_squares(tile, n_t, heads, d, sq, c0):
            for t in range(n_t):
                settle()
                mark(dve.tensor_tensor(sq[:, 0:heads, 0:d], tile(t), tile(t), ALU.mult))
                settle()
                mark(dve.tensor_reduce(sums[:, c0 + t * heads:c0 + (t + 1) * heads], sq[:, 0:heads, 0:d],
                                       AX_X, ALU.add))

        def head_scale(tile, n_t, heads, d, gain, c0):
            for t in range(n_t):
                r = rstd[:, c0 + t * heads:c0 + (t + 1) * heads].unsqueeze(2).to_broadcast([P, heads, d])
                mark(dve.tensor_tensor(tile(t), tile(t), r, ALU.mult))
            settle()
            g = gain.unsqueeze(1).to_broadcast([P, heads, d])
            for t in range(n_t):
                mark(dve.tensor_tensor(tile(t), tile(t), g, ALU.mult))

        def rotate(x1, x2, cos, sin, tmp, heads, half):
            c = cos.unsqueeze(2).to_broadcast([P, NT, heads, half])
            s = sin.unsqueeze(2).to_broadcast([P, NT, heads, half])
            settle()
            mark(dve.tensor_tensor(tmp[0], x1, c, ALU.mult))
            mark(dve.tensor_tensor(tmp[1], x2, s, ALU.mult))
            mark(dve.tensor_tensor(tmp[2], x1, s, ALU.mult))
            mark(dve.tensor_tensor(tmp[3], x2, c, ALU.mult))
            settle()
            mark(dve.tensor_tensor(x1, tmp[0], tmp[1], ALU.subtract))
            mark(dve.tensor_tensor(x2, tmp[2], tmp[3], ALU.add))

        def attention(a, evict_beside):
            side = beside(a.name, a.l, len(a.units))

            def turned(h):
                for what, dst, n in (("q", qT, NT), ("k", kT, a.k_tiles)):
                    key = (a.name, a.l, what, h, 0)
                    bank = aux_wait_full(dve, key)
                    dve.tensor_copy(dst[a.where][0:a.d, h % 2, 0:n * P], bank[0:a.d, 0:n * P])\
                       .then_inc(read_of(key), 1)

            def scores(n):
                h, i = a.units[n]
                keys = a.n_keys(i) * P
                c = (a.first_unit + n) % 64
                key = (a.name, a.l, "S", n)
                bank = aux_wait_full(dve, key)
                if n >= 2:
                    dve.wait_ge(probs_ready, a.first_unit + n - 1)
                dve.tensor_tensor_reduce(out=masked[a.where][:, n % 2, 0:keys], in0=bank[:, 0:keys], in1=a.mask(i),
                                         scale=-a.scale, scalar=3.0e38, op0=ALU.add, op1=ALU.min,
                                         accum_out=neg_max[:, c:c + 1]).then_inc(read_of(key), 1)

            def values(n):
                h, i = a.units[n]
                c = (a.first_unit + n) % 64
                dve.wait_ge(probs_ready, a.first_unit + n + 1)
                mark(dve.reciprocal(row_inv[:, c:c + 1], row_sum[:, c:c + 1]))
                key = (a.name, a.l, "O", n)
                bank = aux_wait_full(dve, key)
                settle()
                dve.tensor_scalar(a.out_of(h, i), bank[:, 0:HD], row_inv[:, c:c + 1], None, ALU.mult)\
                   .then_inc(read_of(key), 1)

            turned(0)
            scores(0)
            for n, (h, i) in enumerate(a.units):
                if i == 1 and h + 1 < a.heads:
                    turned(h + 1)
                if n + 1 < len(a.units):
                    scores(n + 1)
                to = last_step_beside(side, n, a.l, a.name)
                if to is not None:
                    split.to(to + AHEAD)
                for gi in side[n][1]:
                    evict_beside(gi)
                if n:
                    values(n - 1)
            values(len(a.units) - 1)
            aux_wait_read(dve, (a.name, a.l, "O", len(a.units) - 1))

        def update_x(block, l, j):
            gi = gi_of(block, l, "out", j)
            split.through(gi)
            for t in range(NT):
                wait_gemm_full(dve, gi, t)
                xs = x[:, t, j * T:(j + 1) * T]
                dve.tensor_tensor(xs, gemm_bank[t][:, :], xs, ALU.add).then_inc(gemm_read[t], 1)

        def rope_angles():
            flat = [angle[:, i, :, :].rearrange("p t f -> p (t f)") for i in range(4)]
            for t in range(NT):
                mark(dve.tensor_scalar(angle[:, 0, t, :], inv_freq[:, :], vec_col(R_POS + t), None, ALU.mult))
            settle()
            mark(dve.tensor_scalar(flat[1], flat[0], 1.0 / TWO_PI, ROUND, ALU.mult, ALU.add))
            settle()
            mark(dve.tensor_scalar(flat[1], flat[1], ROUND, None, ALU.subtract))
            for part in (PI_1, PI_2, PI_3):
                settle()
                mark(dve.scalar_tensor_tensor(out=flat[0], in0=flat[1], scalar=-part, in1=flat[0],
                                              op0=ALU.mult, op1=ALU.add))
            settle()
            mark(dve.tensor_scalar(flat[0], flat[0], math.pi * (1 - 2 ** -23), -math.pi * (1 - 2 ** -23),
                                   ALU.min, ALU.max))
            settle()
            mark(dve.tensor_scalar(flat[1], flat[0], math.pi / 2, None, ALU.add))
            settle()
            mark(dve.tensor_scalar(flat[2], flat[1], math.pi, -TWO_PI, ALU.is_gt, ALU.mult))
            settle()
            mark(dve.tensor_tensor(flat[1], flat[1], flat[2], ALU.add))
            settle()
            dve.tensor_scalar(flat[1], flat[1], math.pi * (1 - 2 ** -23), -math.pi * (1 - 2 ** -23),
                              ALU.min, ALU.max).then_inc(rope_ready, 1)

        def block_1(l):
            job = 5 * l
            if l:
                for j in range(2):
                    wait_gemm_read(dve, gi_of(1, l - 1, "out", j))
            scale_rows(x, x_n[0], NT, job + 1)
            if l == 0:
                rope_angles()
                split.to(RING)
            features((1, l, "x"), KD, T, act_hi, act_lo, vec_col(R_X + KD * l, KD))
            split.through(gi_of(1, l, "c"))
            wait_gemm_read(dve, gi_of(1, l, "c"))
            for t in range(NT):
                for n, (a, b) in enumerate(((0, QR), (QR, QR + KVR))):
                    settle()
                    ins = dve.tensor_tensor_reduce(out=c_sq[:, a:b], in0=c_tok[:, t, a:b], in1=c_tok[:, t, a:b],
                                                   scale=1.0 / (b - a), scalar=0.0, op0=ALU.mult, op1=ALU.add,
                                                   accum_out=sums[:, 8 + n * NT + t:9 + n * NT + t])
                    if t < NT - 1 or n == 0:
                        mark(ins)
                    else:
                        ins.then_inc(sums_ready, 1)
            split.through(gi_of(1, l, "v"))
            dve.wait_ge(rstd_ready, job + 2)
            for t in range(NT):
                for n, (a, b) in enumerate(((0, QR), (QR, QR + KVR))):
                    ins = dve.tensor_scalar(c_tok[:, t, a:b], c_tok[:, t, a:b],
                                            rstd[:, 8 + n * NT + t:9 + n * NT + t], None, ALU.mult)
                    if t < NT - 1 or n == 0:
                        mark(ins)
                    else:
                        ins.then_inc(c_scaled, 1)
            wait_gemm_read(dve, gi_of(1, l, "v"))
            for t in range(NT):
                mark(dve.bn_stats(stats6[:, t, :], vn[:, t, :]))
            settle()
            for t in range(NT):
                ins = dve.bn_aggr(mean_var[:, t, :], stats6[:, t, :])
                if t < NT - 1:
                    mark(ins)
                else:
                    ins.then_inc(sums_ready, 1)
            split.through(gi_of(1, l, "u"))
            features((1, l, "c"), 3, T, c_hi, c_lo, vec_col(R_C + 3 * l, 3))
            dve.wait_ge(sg_loaded, 64 * (l + 1))
            dve.wait_ge(rstd_ready, job + 3)
            for t in range(NT):
                mark(dve.tensor_scalar(vn[:, t, :], vn[:, t, :], mean_var[:, t, 0:1], rstd[:, t:t + 1],
                                       ALU.subtract, ALU.mult))
            settle()
            for t in range(NT):
                mark(dve.tensor_tensor(vn[:, t, :], vn[:, t, :], ln_g[:, :], ALU.mult))
            settle()
            for t in range(NT):
                ins = dve.tensor_tensor(vn[:, t, :], vn[:, t, :], ln_b[:, :], ALU.add)
                if t < NT - 1:
                    mark(ins)
                else:
                    ins.then_inc(vn_ready, 1)
            key = (1, l, "sgw", 0)
            bank = aux_wait_full(dve, key)
            view = bank[:, :].rearrange("p (g i) -> p g i", g=4)
            mark(dve.memset(sg_wT[CHUNK:P, :, 0:CHUNK], 0.0))
            mark(dve.tensor_copy(sg_wT[0:CHUNK, :, :], view[0:CHUNK, :, :]))
            dve.tensor_copy(sg_wT[CHUNK:P, :, CHUNK:P], view[CHUNK:P, :, CHUNK:P]).then_inc(read_of(key), 1)
            split.through(gi_of(1, l, "za"))
            wait_gemm_read(dve, gi_of(1, l, "u"))
            wait_gemm_read(dve, gi_of(1, l, "za"))
            for g in range(4):
                mark(dve.tensor_tensor(u[:, g, :], u[:, g, :], za[:, g, :], ALU.mult))
            split.through(gi_of(1, l, "zb"))
            for g in range(4):
                key = (1, l, "sv", g)
                bank = aux_wait_full(dve, key)
                bias = sg_bias[:, g, :].unsqueeze(1).to_broadcast([P, NT, P])
                dve.tensor_tensor(za[:, g, :].rearrange("p (n i) -> p n i", n=NT),
                                  bank[:, :].rearrange("p (n i) -> p n i", n=NT), bias,
                                  ALU.add).then_inc(read_of(key), 1)
            settle()
            for g in range(4):
                aux_wait_read(dve, (1, l, "sv", g))
                dve.tensor_tensor(u[:, g, :], u[:, g, :], za[:, g, :], ALU.mult).then_inc(ya_ready, 1)
            for g in range(4):
                dve.wait_ge(ya_hi_ready, 4 * l + g + 1)
                dve.tensor_tensor(y_lo[0][:, g, :], u[:, g, :], y_hi[0][:, g, :].bitcast(F32),
                                  ALU.subtract).then_inc(ya_lo_ready, 1)
            for i in range(2):
                split.through(gi_of(1, l, "uq", i))
            for i in range(2):
                gi = gi_of(1, l, "ukv", i)
                split.through(gi)
                for b in range(NT):
                    wait_gemm_full(dve, gi, b)
                    kv = gemm_bank[b][:, :].rearrange("p (h c) -> p h c", h=4)
                    mark(dve.tensor_copy(k[:, b, 4 * i:4 * i + 4, 0:NOPE], kv[:, :, 0:NOPE]))
                    dve.tensor_copy(v_mla[:, b, 4 * i:4 * i + 4, :], kv[:, :, NOPE:NOPE + MV])\
                       .then_inc(gemm_read[b], 1)
            for t in range(NT):
                mark(dve.tensor_copy(k[:, t, :, NOPE:QK],
                                     c_tok[:, t, QR + KVR:NC_C].unsqueeze(1).to_broadcast([P, MH, ROPE])))
            for i in range(2):
                wait_gemm_read(dve, gi_of(1, l, "uq", i))
                wait_gemm_read(dve, gi_of(1, l, "ukv", i))
            head_squares(lambda t: q[:, t, :, :], NT, MH, QK, sq_1, 0)
            head_squares(lambda t: k[:, t, :, :], NT, MH, QK, sq_1, NT * MH)
            settle()
            dve.engine_nop().then_inc(sums_ready, 1)
            dve.wait_ge(rstd_ready, job + 4)
            head_scale(lambda t: q[:, t, :, :], NT, MH, QK, gain_q[:, l, :], 0)
            head_scale(lambda t: k[:, t, :, :], NT, MH, QK, gain_k[:, l, :], NT * MH)
            if l == 0:
                dve.wait_ge(sines_ready, 2)
            for tile in (q, k):
                rotate(tile[:, :, :, NOPE:NOPE + HALF], tile[:, :, :, NOPE + HALF:QK], cos1[:, :, :], sin1[:, :, :],
                       [r[:, :, :, :] for r in rope_1], MH, HALF)
            settle()
            dve.engine_nop().then_inc(heads_ready, 1)

            def beside_mla(gi):
                dst = {(1, l, "qkc"): lambda b: qk_c[:, b, :], (1, l, "vc"): lambda b: vc[:, b, :],
                       (1, l, "zc"): lambda b: zc[:, b, :]}.get(group_key[gi])
                if dst:
                    evict_now(gi, dst)
                else:
                    wait_gemm_full(dve, gi, 0)
                    dve.tensor_copy(g_T[:, :], gemm_bank[0][0:GR, :]).then_inc(gemm_read[0], 1)

            attention(attention_1(l), beside_mla)
            z = zb[:, :, :].rearrange("p t (h d) -> p t h d", h=MH)
            wait_gemm_read(dve, gi_of(1, l, "zb"))
            for t in range(NT):
                dve.tensor_tensor(yb_tok[:, t, :].rearrange("p (h d) -> p h d", h=MH), q[:, t, :, 0:MV],
                                  z[:, t, :, :], ALU.mult)\
                   .then_inc(rows_gated, 1)
            features((1, l, "yb"), 4, T, y_hi[1], y_lo[1])
            gla(l)
            for j in range(2):
                for i in range(3):
                    n = 3 * j + i
                    split.through(gi_of(1, l, ("gate", j, i)))
                    gi = gi_of(1, l, "branch", j, i)
                    split.through(gi)
                    for m in range(4):
                        wait_gemm_read(dve, gi_of(1, l, ("gate", j, i)), m)
                        wait_gemm_full(dve, gi, m)
                        mm = merged[:, 4 * j + m, :]
                        dst = mm if i == 0 else product[:, m % 2, :]
                        dve.tensor_tensor(dst, gemm_bank[m][:, :], gate[:, n % 2, m, :], ALU.mult)\
                           .then_inc(gemm_read[m], 1)
                        if i:
                            wait_gemm_read(dve, gi, m)
                            ins = dve.tensor_tensor(mm, mm, product[:, m % 2, :], ALU.add)
                            if i == 2:
                                ins.then_inc(merged_ready, 1)
                            else:
                                mark(ins)
                    settle()
            for kk in range(KD):
                dve.wait_ge(merged_hi_ready, KD * l + kk + 1)
                dve.tensor_tensor(act_lo[:, kk, :], merged[:, kk, :], act_hi[:, kk, :].bitcast(F32),
                                  ALU.subtract).then_inc(merged_lo_ready, 1)
            for j in range(2):
                update_x(1, l, j)

        def gla(l):
            for m in range(2):
                key = (1, l, "gl", m)
                bank = aux_wait_full(dve, key)
                dve.tensor_scalar(log_a[:, m, :], bank[:, :], vec_col(R_GLA + 2 * l + m), None, ALU.add)\
                   .then_inc(read_of(key), 1)
            for m in range(2):
                aux_wait_read(dve, (1, l, "gl", m))
            dve.scalar_tensor_tensor(out=log_t[:, :, :], in0=log_a[:, :, :], scalar=-1.0, in1=log_a[:, :, :],
                                     op0=ALU.mult, op1=ALU.min).then_inc(gla_gate, 1)
            dve.wait_ge(gla_exp, 4 * l + 1)
            mark(dve.scalar_tensor_tensor(out=log_a[:, :, :], in0=log_a[:, :, :], scalar=0.0, in1=log_t[:, :, :],
                                          op0=ALU.min, op1=ALU.subtract))
            dve.wait_ge(gla_loaded, 32 * (l + 1))
            settle()
            mark(dve.tensor_tensor_scan(b_cum[:, 0, :], carry[:, :], log_a[:, 0, :], 0.0, ALU.mult, ALU.add))
            dve.tensor_tensor_scan(b_cum[:, 1, :], carry[:, :], log_a[:, 1, :], 0.0, ALU.mult, ALU.add)\
               .then_inc(gla_gate, 1)
            dve.wait_ge(gla_gate, 3 * l + 2)
            chunks = b_cum[:, :, :].rearrange("p m (n c) -> p (m n) c", c=CHUNK)
            dve.tensor_tensor(e_st[:, :, :].rearrange("p m (n c) -> p (m n) c", c=CHUNK),
                              chunks[:, :, CHUNK - 1:CHUNK].to_broadcast([P, 2 * T // CHUNK, CHUNK]), chunks,
                              ALU.subtract).then_inc(gla_gate, 1)
            dve.wait_ge(gla_exp, 4 * l + 2)
            mark(dve.scalar_tensor_tensor(out=qk_c[:, 0:2, :], in0=qk_c[:, 0:2, :], scalar=DK ** -0.5,
                                          in1=e_up[:, :, :], op0=ALU.mult, op1=ALU.mult))
            mark(dve.tensor_copy(decay[:, :, :], e_up[:, :, CHUNK - 1:T:CHUNK]))
            dve.wait_ge(gla_exp, 4 * l + 3)
            dve.wait_ge(pads_zeroed, 2 * l + 1)
            for hh in range(2):
                r = slice(hh * DK, (hh + 1) * DK)
                ins = dve.tensor_tensor(kt_pad[r, :, hh, :], qk_c[r, 2:4, :], e_dn[r, :, :], ALU.mult)
                if hh:
                    ins.then_inc(gla_qk, 1)
                else:
                    mark(ins)
            dve.wait_ge(gla_exp, 4 * l + 4)
            dve.wait_ge(gla_qk, 2 * l + 1)
            settle()
            dve.tensor_tensor(qk_c[:, 2:4, :], qk_c[:, 2:4, :], e_st[:, :, :], ALU.mult).then_inc(gla_qk, 1)
            for m in range(2):
                key = (1, l, "ks", m)
                bank = aux_wait_full(dve, key)
                dve.tensor_copy(ks_tok[:, :, m * P:(m + 1) * P], bank[:, :].rearrange("p (t c) -> p t c", t=NT))\
                   .then_inc(read_of(key), 1)
            dve.wait_ge(pads_zeroed, 2 * l + 2)
            for h in range(GH):
                key = (1, l, "att", h)
                bank = aux_wait_full(dve, key)
                dve.copy_predicated(att[:, h, :, :], keep[:, :, :], bank[:, :].rearrange("p (t i) -> p t i", t=NT))\
                   .then_inc(read_of(key), 1)
            for n in range(T // CHUNK - 1):
                key = (1, l, "U", n)
                bank = aux_wait_full(dve, key)
                settle()
                if n:
                    aux_wait_read(dve, (1, l, "U", n - 1))
                for m in range(2):
                    for hh in range(2):
                        r = slice(hh * DK, (hh + 1) * DK)
                        c = slice(hh * DV, (hh + 1) * DV)
                        new = bank[r, m * 2 * DV + hh * DV:m * 2 * DV + (hh + 1) * DV]
                        if n == 0:
                            ins = dve.tensor_copy(state[r, 0, m, c], new)
                        else:
                            ins = dve.scalar_tensor_tensor(out=state[r, n, m, c], in0=state[r, n - 1, m, c],
                                                           scalar=decay[r, m, n:n + 1], in1=new,
                                                           op0=ALU.mult, op1=ALU.add)
                        if m and hh:
                            ins.then_inc(read_of(key), 1)
                        else:
                            mark(ins)
            heads = lambda t: o_tok[:, t, :].rearrange("p (h e) -> p h e", h=GH)
            for t in range(NT):
                aux_wait_read(dve, (1, l, "o", t))
            head_squares(heads, NT, GH, DV, o_sq[:, :].rearrange("p (h e) -> p h e", h=GH), 0)
            settle()
            dve.engine_nop().then_inc(sums_ready, 1)
            dve.wait_ge(rstd_ready, 5 * l + 5)
            head_scale(heads, NT, GH, DV, gain_o[:, l, :], 0)
            dve.wait_ge(silu_ready, NT * (l + 1))
            settle()
            for t in range(NT):
                dve.tensor_tensor(o_tok[:, t, :], o_tok[:, t, :], zc[:, t, :], ALU.mult).then_inc(rows_gated, 1)
            features((1, l, "yc"), 4, T, y_hi[2], y_lo[2])

        def block_2(l):
            job = 5 * DEPTH + 4 * l
            prev = (1, DEPTH - 1) if l == 0 else (2, l - 1)
            for j in range(2):
                wait_gemm_read(dve, gi_of(*prev, "out", j))
            scale_rows(mem_x, mem_n, NMEM // P, job + 1, NT)
            scale_rows(x, x_n[1], NT, job + 1)
            features((2, l, "mem"), KD, NMEM, mem_hi, mem_lo, vec_col(R_MEM + KD * l, KD))
            split.through(gi_of(2, l, "mkv"))
            features((2, l, "x"), KD, T, act_hi, act_lo, vec_col(R_X + KD * (DEPTH + l), KD))
            for name in ("aq", "ak", "av"):
                split.through(gi_of(2, l, name))

            def heads(tiles, job_n, rope):
                c0 = 0
                for tile, n_t, n_h, gain in tiles:
                    head_squares(tile, n_t, n_h, HD, sq_2, c0)
                    c0 += n_t * n_h
                settle()
                dve.engine_nop().then_inc(sums_ready, 1)
                dve.wait_ge(rstd_ready, job_n)
                c0 = 0
                for tile, n_t, n_h, gain in tiles:
                    head_scale(tile, n_t, n_h, HD, gain_2[:, l, gain, :], c0)
                    c0 += n_t * n_h
                for tile in rope:
                    rotate(tile[:, :, :, 0:HD // 2], tile[:, :, :, HD // 2:HD], cos2[:, :, :], sin2[:, :, :],
                           [r[:, :, :, :] for r in rope_2], AH, HD // 2)
                settle()
                dve.engine_nop().then_inc(heads_ready, 1)

            def kind_heads(a, gain, job_n):
                for n in ("q", "k"):
                    wait_gemm_read(dve, gi_of(2, l, a + n))
                heads([(lambda t: kinds[a + "q"][:, t, :, :], NT, AH, gain),
                       (lambda t: kinds[a + "k"][:, t, :, :], NT, AH, gain + 1)], job_n,
                      [kinds[a + "q"], kinds[a + "k"]])

            def beside_2(gi):
                evict_now(gi, lambda b: flat_2(group_key[gi][2])[:, b, :])

            kind_heads("a", 0, job + 2)
            attention(attention_2(l, "moba"), beside_2)
            kind_heads("b", 2, job + 3)
            attention(attention_2(l, "dilated"), beside_2)
            wait_gemm_read(dve, gi_of(2, l, "mkv"))
            wait_gemm_read(dve, gi_of(2, l, "m"))
            heads([(lambda t: m_tok[:, t, 0, :, :], NT, EH, 4),
                   (lambda t: mkv[:, t, 0, :, :], NMEM // P, EH, 5)], job + 4, [])
            attention(attention_2(l, "memory"), beside_2)
            for n, (y, g, c0, width) in enumerate((("aq", "ag", 0, WA), ("bq", "bg", 0, WB), ("m", "m", WE, WE))):
                dve.wait_ge(silu_ready, NT * DEPTH + 3 * l + n + 1)
                for t in range(NT):
                    rows = flat_2(y)[:, t, 0:width]
                    dve.tensor_tensor(rows, rows, flat_2(g)[:, t, c0:c0 + width], ALU.mult).then_inc(rows_gated, 1)
            for name, tiles, k0 in (("aq", 3, 0), ("bq", 3, 3), ("m", 2, 6)):
                features((2, l, "y" + name), tiles, T, act_hi, act_lo, None, k0)
            for j in range(2):
                update_x(2, l, j)

        dve.wait_ge(consts_loaded, 16 * N_CONST)
        dve.tensor_copy(vec_rows[R_POS:R_POS + NT, :], pos_rows[R_POS:R_POS + NT, :]).then_inc(positions_ready, 1)
        bank = aux_wait_full(dve, "vec")
        dve.tensor_copy(vec_cols[:, :], bank[:, 0:N_ROWS]).then_inc(read_of("vec"), 1)
        aux_wait_read(dve, "vec")
        for l in range(DEPTH):
            block_1(l)
        for l in range(DEPTH):
            block_2(l)

    @block.gpsimd
    def _(pool):
        marks = [0]

        def mark(ins):
            ins.then_inc(pool_done, 1)
            marks[0] += 1

        def factors(source, c0, n, scale):
            mark(pool.tensor_scalar(mean_sq[:, c0:c0 + n], source, scale, EPS, ALU.mult, ALU.add))
            pool.wait_ge(pool_done, marks[0])
            pool.tensor_tensor(rstd[:, c0:c0 + n], mean_sq[:, c0:c0 + n], minus_half[:, 0:n], ALU.pow)\
                .then_inc(rstd_ready, 1)

        mark(pool.memset(minus_half[:, :], -0.5))
        pool.wait_ge(pool_done, marks[0])
        for l in range(DEPTH):
            pool.wait_ge(squares_ready, NT * (l + 1))
            factors(sums[:, 0:NT], 0, NT, 1.0)
            pool.wait_ge(sums_ready, 4 * l + 1)
            factors(sums[:, 8:8 + 2 * NT], 8, 2 * NT, 1.0)
            pool.wait_ge(sums_ready, 4 * l + 2)
            factors(mean_var[:, :, 1], 0, NT, 1.0)
            pool.wait_ge(sums_ready, 4 * l + 3)
            factors(sums[:, 0:64], 0, 64, 1.0 / QK)
            aux_wait_read(pool, (1, l, "yb", 3))
            pool.memset(kt_pad[:, :, :, :], 0.0).then_inc(pads_zeroed, 1)
            pool.wait_ge(gla_qk, 2 * l + 2)
            mark(pool.memset(att[:, :, :, :], 0.0))
            pool.memset(state[:, :, :, :], 0.0).then_inc(pads_zeroed, 1)
            pool.wait_ge(sums_ready, 4 * l + 4)
            factors(sums[:, 0:NT * GH], 0, NT * GH, 1.0 / DV)
        for l in range(DEPTH):
            pool.wait_ge(squares_ready, NT * DEPTH + (NT + NMEM // P) * (l + 1))
            factors(sums[:, 0:NT + NMEM // P], 0, NT + NMEM // P, 1.0)
            for n, width in enumerate((2 * NT * AH, 2 * NT * BH, (NT + NMEM // P) * EH)):
                pool.wait_ge(sums_ready, 4 * DEPTH + 3 * l + n + 1)
                factors(sums[:, 0:width], 0, width, 1.0 / HD)

    @block.sync
    def _(sp):
        def load_piece(p):
            gi, k0, k1 = pieces[p]
            g = groups[gi]
            if p >= RAW:
                old_gi, _, old_k1 = pieces[p - RAW]
                sp.wait_ge(w_lo_ready, first_step[old_gi] + old_k1)
            sp.dma_start(raw[:, p % RAW, 0:k1 - k0, 0:g.n], g.src(k0, k1).rearrange("(k p) n -> p k n", p=P))\
              .then_inc(raw_loaded[p % RAW], 16)

        sp.dma_start(x[:, :, :], w["x"][0].rearrange("(t p) d -> p t d", p=P)).then_inc(x_loaded, 16)
        for dst, src in const_loads:
            sp.dma_start(dst, src).then_inc(consts_loaded, 16)
        for p in range(len(pieces)):
            load_piece(p)
        for j in range(2):
            wait_gemm_read(sp, gi_of(2, DEPTH - 1, "out", j))
            sp.dma_start(out[0].rearrange("(t p) d -> p t d", p=P)[:, :, j * T:(j + 1) * T],
                         x[:, :, j * T:(j + 1) * T]).then_inc(out_stored, 16)
        sp.wait_ge(out_stored, 32)


_INS = ["x", "positions", "norm_g", "w_in", "b_gate", "sg_ln_g", "sg_ln_b", "sg_w", "sg_b", "mla_cq_g", "mla_ckv_g",
        "mla_w_uq", "mla_w_ukv", "mla_q_g", "mla_k_g", "gla_w_gate", "gla_b_gate", "gla_o_g", "w_branch", "w_out",
        "mem_2", "norm_g_2", "w_in_2", "w_out_2", "mem_norm_g_2", "w_mem_kv_2", "qk_g_2"]


def kernel(**inputs):
    import concourse.bacc as bacc
    from concourse.bass_utils import run_bass_kernel_spmd

    nc = bacc.Bacc("TRN2", target_bir_lowering=False, num_devices=1)
    given = {name: np.ascontiguousarray(inputs[name]) for name in _INS}
    given.update(constants())
    w = {name: nc.dram_tensor(f"in_{name}", a.shape, mybir.dt.from_np(a.dtype), kind="ExternalInput").ap()
         for name, a in given.items()}
    out = nc.dram_tensor("out_x", (1, T, D), F32, kind="ExternalOutput").ap()
    with ExitStack() as stack:
        hybrid_kernel(nc, w, out, stack)
    r = run_bass_kernel_spmd(nc, [{f"in_{name}": a for name, a in given.items()}], core_ids=[0])
    return r.results[0]["out_x"]
```

```python
import math
from contextlib import ExitStack

import numpy as np
import concourse.bass as bass
from concourse import mybir

F32 = mybir.dt.float32
F32R = mybir.dt.float32r
I32 = mybir.dt.int32
ALU = mybir.AluOpType
ACT = mybir.ActivationFunctionType
AX_X = mybir.AxisListType.X

P = 128
T = 512
NT = T // P
D = 1024
KD = D // P
DEPTH = 2
EPS = 1e-6
NEG = -1.0e30

CHUNK = 64
BW = 512
MH, NOPE, ROPE, MV = 8, 64, 32, 64
QK = NOPE + ROPE
HALF = ROPE // 2
QR, KVR = 256, 128
GH, DK, DV, GR, TAU = 4, 64, 128, 16, 16.0
C_U, C_V, C_ZA = 0, BW, 2 * BW
C_C = 3 * BW
NC_C = QR + KVR + ROPE
C_ZB = C_C + NC_C
C_QC = C_ZB + MH * MV
C_VC = C_QC + 2 * GH * DK
C_GC = C_VC + GH * DV
C_ZC = C_GC + GR
C_GATE = C_ZC + GH * DV

HD = 64
AH, BH, EH = 6, 6, 4
NMEM = 256
WA, WB, WE = AH * HD, BH * HD, EH * HD

TWO_PI = 2.0 * math.pi
PI_1 = 6.28125
PI_2 = float((np.array([np.float32(TWO_PI - PI_1)]).view(np.uint32) & np.uint32(0xFFFFF000)).view(np.float32)[0])
PI_3 = float(np.float32(TWO_PI - PI_1 - PI_2))
ROUND = 12582912.0

RING = 4
AHEAD = RING - 1
RAW = 4
PIECE = 2


def constants():
    p = np.arange(P)[:, None]
    c = np.arange(T)[None, :]
    d = (T - P) + p - c
    diag = c - (T - P)
    out = {}
    out["k_ident"] = np.eye(P, dtype=np.float32)
    out["k_mask_chunk"] = np.where((diag >= 0) & (diag // CHUNK > p // CHUNK), NEG, 0.0).astype(np.float32)
    out["k_mask_causal"] = np.where(d < 0, NEG, 0.0).astype(np.float32)
    count = ((d >= 0) & (d <= 128)).astype(int) + ((d >= 0) & (d % 4 == 0)) + ((d >= 0) & (d % 16 == 0))
    bias = np.where(count > 0, np.log(np.maximum(count, 1)) / (HD ** -0.5), NEG)
    out["k_mask_dilated"] = bias.astype(np.float32)
    j, i = np.arange(P)[:, None], np.arange(P)[None, :]
    keep = ((j <= i) & (j // CHUNK == i // CHUNK)).astype(np.int32)
    out["k_keep"] = np.tile(keep, (1, NT)).astype(np.int32)
    out["k_carry"] = np.tile((np.arange(T) % CHUNK != 0).astype(np.float32), (P, 1))
    inv = (np.float32(1.0) / np.power(np.float32(10000.0), np.arange(HALF, dtype=np.float32) * np.float32(2.0)
                                      / np.float32(ROPE))).astype(np.float32)
    out["k_inv"] = np.tile(inv, (P, 1)).astype(np.float32)
    inv2 = np.power(np.float32(10000.0), -np.arange(HD // 2, dtype=np.float32) / np.float32(HD // 2)).astype(np.float32)
    ang = np.arange(T, dtype=np.float32)[:, None] * inv2[None, :]
    out["k_cos2"] = np.cos(ang).astype(np.float32)
    out["k_sin2"] = np.sin(ang).astype(np.float32)
    return out


class Group:

    def __init__(self, src, K, n, banks):
        self.src, self.K, self.n, self.banks = src, K, n, banks


def plan_groups(w):
    groups, index = [], {}

    def add(key, src, K, n, banks):
        index[key] = len(groups)
        groups.append(Group(src, K, n, banks))

    def cols(name, l, c0, n):
        return lambda k0, k1: w[name][l, k0 * P:k1 * P, c0:c0 + n]

    for l in range(DEPTH):
        def one(tag, c0, n, banks=4):
            add((1, l, tag), cols("w_in", l, c0, n), KD, n, banks)
        one("c", C_C, NC_C)
        one("v", C_V, BW)
        for i in range(2):
            add((1, l, "uq", i), cols("mla_w_uq", l, i * 4 * QK, 4 * QK), QR // P, 4 * QK, 4)
        for i in range(2):
            add((1, l, "ukv", i), cols("mla_w_ukv", l, i * 4 * (NOPE + MV), 4 * (NOPE + MV)), 1, 4 * (NOPE + MV), 4)
        one("u", C_U, BW)
        one("za", C_ZA, BW)
        one("zb", C_ZB, MH * MV)
        one("qkc", C_QC, 2 * GH * DK)
        one("gc", C_GC, P, 1)
        one("vc", C_VC, GH * DV)
        one("zc", C_ZC, GH * DV)
        for j in range(2):
            for i in range(3):
                one(("gate", j, i), C_GATE + i * D + j * T, T)
                def branch(k0, k1, i=i, j=j, l=l):
                    return w["w_branch"][l, i, k0 * P:k1 * P, j * T:(j + 1) * T]
                add((1, l, "branch", j, i), branch, BW // P, T, 4)
        for j in range(2):
            add((1, l, "out", j), cols("w_out", l, j * T, T), KD, T, 4)
    for l in range(DEPTH):
        def two(tag, c0, n, banks=4, name="w_in_2"):
            add((2, l, tag), cols(name, l, c0, n), KD, n, banks)
        two("mkv", 0, 2 * WE, NMEM // P, "w_mem_kv_2")
        two("aq", 0, WA)
        two("ak", WA, WA)
        two("av", 2 * WA, WA)
        two("bq", 4 * WA, WB)
        two("bk", 4 * WA + WB, WB)
        two("bv", 4 * WA + 2 * WB, WB)
        two("m", 4 * WA + 4 * WB, 2 * WE)
        two("ag", 3 * WA, WA)
        two("bg", 4 * WA + 3 * WB, WB)
        for j in range(2):
            add((2, l, "out", j), cols("w_out_2", l, j * T, T), KD, T, 4)
    return groups, index


def hybrid_kernel(nc, w, out, stack):
    groups, gindex = plan_groups(w)
    first_step, step_group = [], []
    first_piece, pieces = [], []
    for gi, g in enumerate(groups):
        first_step.append(len(step_group))
        first_piece.append(len(pieces))
        step_group += [(gi, k) for k in range(g.K)]
        pieces += [(gi, k0, min(g.K, k0 + PIECE)) for k0 in range(0, g.K, PIECE)]
    bank_use, bank_uses = {}, [0] * 4
    for gi, g in enumerate(groups):
        for b in range(g.banks):
            bank_use[gi, b] = bank_uses[b]
            bank_uses[b] += 1
    steps_marked = []
    for s, (gi, k) in enumerate(step_group):
        steps_marked.append((steps_marked[-1] if s else 0) + (k != groups[gi].K - 1))

    SBUF_0 = 16512
    KB = 1024
    top = [SBUF_0]

    def at(name, shape, dt, offset):
        return nc.alloc_sbuf_tensor_at(name, shape, dt, offset=offset)

    def place(name, shape, dt=F32):
        size = 4 * int(np.prod(shape[1:]))
        t = at(name, shape, dt, top[0])
        top[0] += (size + 31) // 32 * 32
        return t

    def area(size):
        a = top[0]
        top[0] += size
        return a

    x = place("x", [P, NT, D])
    act_hi = place("act_hi", [P, KD, T], F32R)
    act_lo = place("act_lo", [P, KD, T], F32R)
    raw = place("raw", [P, RAW, PIECE, T])
    w_hi = place("w_hi", [P, RING, T], F32R)
    w_lo = place("w_lo", [P, RING, T], F32R)
    ident = place("ident", [P, P])
    mask_chunk = place("mask_chunk", [P, T])
    mask_causal = place("mask_causal", [P, T])
    mask_dilated = place("mask_dilated", [P, T])
    inv_freq = place("inv_freq", [P, HALF])
    cos1 = place("cos1", [P, NT, HALF])
    sin1 = place("sin1", [P, NT, HALF])
    cos2 = place("cos2", [P, NT, HD // 2])
    sin2 = place("sin2", [P, NT, HD // 2])
    minus_half = place("minus_half", [P, 64])
    R_GATE, R_X, R_MEM, R_POS, R_C, R_GLA = 0, 48, 80, 96, 100, 106
    N_ROWS = 110
    vec_cols = place("vec_cols", [P, N_ROWS])
    w_gu = place("w_gu", [GR, DEPTH, GH * DK])
    gain_q = place("gain_q", [P, DEPTH, QK])
    gain_k = place("gain_k", [P, DEPTH, QK])
    gain_o = place("gain_o", [P, DEPTH, DV])
    gain_2 = place("gain_2", [P, DEPTH, 6, HD])
    sums = place("sums", [P, 72])
    mean_sq = place("mean_sq", [P, 72])
    rstd = place("rstd", [P, 72])
    head_sums = place("head_sums", [P, 64])
    head_rstd = place("head_rstd", [P, 64])
    newton = place("newton", [P, 64])
    stats6 = place("stats6", [P, NT, 6])
    mean_var = place("mean_var", [P, NT, 2])
    neg_max = place("neg_max", [P, 64])
    row_sum = place("row_sum", [P, 64])
    row_inv = place("row_inv", [P, 64])

    Y = area(48 * KB)
    A = area(0)
    END = 229344
    assert A + 60 * KB <= END, (A, END, (END - A) / 1024)

    vec_rows = at("vec_rows", [P, P], F32, A)
    pos_rows = at("pos_rows", [P, P], I32, A + KB)
    angle = at("angle", [P, 4, NT, HALF], F32, A + 8 * KB)
    y_hi = [at(f"y{i}_hi", [P, 4, T], F32R, Y + 16 * KB * i) for i in range(3)]
    y_lo = [at(f"y{i}_lo", [P, 4, T], F32R, Y + 16 * KB * i + 8 * KB) for i in range(3)]
    zb = at("zb", [P, NT, MH * MV], F32, Y + 16 * KB)
    v_mla = at("v_mla", [P, NT, MH, MV], F32, Y + 24 * KB)
    za = at("za", [P, 4, T], F32, Y + 32 * KB)
    vn = at("vn", [P, NT, BW], F32, Y + 40 * KB)
    vc = at("vc", [P, NT, GH * DV], F32, Y + 32 * KB)
    zc = at("zc", [P, NT, GH * DV], F32, Y + 40 * KB)
    u = at("u", [P, 4, T], F32, A)
    qk_c = at("qk_c", [P, 4, T], F32, A)
    q = at("q", [P, NT, MH, QK], F32, A + 8 * KB)
    k = at("k", [P, NT, MH, QK], F32, A + 20 * KB)
    sg_w_raw = at("sg_w_raw", [P, 4, P], F32, Y)
    sg_wT = at("sg_wT", [P, 4, P], F32, Y + 2 * KB)
    sg_bias = at("sg_bias", [P, 4, P], F32, Y + 4 * KB)
    ln_g = at("ln_g", [P, BW], F32, Y + 6 * KB)
    ln_b = at("ln_b", [P, BW], F32, Y + 8 * KB)
    W1 = A + 32 * KB
    yb_tok = at("yb_tok", [P, NT, MH * MV], F32, W1 + 8 * KB)
    c_tok = at("c_tok", [P, NT, NC_C], F32, W1)
    c_sq = at("c_sq", [P, NC_C], F32, W1 + 6784)
    c_hi = at("c_hi", [P, 3, T], F32R, W1 + 9 * KB)
    c_lo = at("c_lo", [P, 3, T], F32R, W1 + 15 * KB)
    sq_1 = at("sq_1", [P, 2, MH, QK], F32, W1 + 6784)
    rope_1 = [at(f"rope_1{i}", [P, NT, MH, HALF], F32, W1 + 13 * KB + 2 * KB * i) for i in range(4)]
    table_1 = at("table_1", [P, 4, NT, HALF], F32, A + 56 * KB)
    g_T = at("g_T", [GR, T], F32, A + 54 * KB)
    x_n = [at("x_n1", [P, NT, D], F32, W1), at("x_n2", [P, NT, D], F32, Y)]
    squared = at("squared", [P, 2, NT, T], F32, Y + 32 * KB)
    merged = at("merged", [P, KD, T], F32, A)
    gate = at("gate", [P, 2, 4, T], F32, A + 16 * KB)
    product = at("product", [P, 2, T], F32, A + 32 * KB)
    merged_hi = [at("merged_hi0", [P, 4, T], F32R, A + 36 * KB), at("merged_hi1", [P, 4, T], F32R, Y)]
    merged_lo = [at("merged_lo0", [P, 4, T], F32R, A + 44 * KB), at("merged_lo1", [P, 4, T], F32R, Y + 8 * KB)]
    kt_pad = at("kt_pad", [P, 2, 2, T], F32, A + 8 * KB)
    ks_tok = at("ks_tok", [P, NT, GH * DK], F32, A + 16 * KB)
    keep = at("keep", [P, NT, P], I32, A + 20 * KB)
    carry = at("carry", [P, T], F32, A + 22 * KB)
    log_a = at("log_a", [P, 2, T], F32, A + 24 * KB)
    log_t = at("log_t", [P, 2, T], F32, A + 28 * KB)
    b_cum = at("b_cum", [P, 2, T], F32, A + 32 * KB)
    e_up = at("e_up", [P, 2, T], F32, A + 36 * KB)
    e_dn = at("e_dn", [P, 2, T], F32, A + 40 * KB)
    e_st = at("e_st", [P, 2, T], F32, A + 44 * KB)
    att = at("att", [P, GH, NT, P], F32, A + 24 * KB)
    state = at("state", [P, T // CHUNK - 1, 2, 2 * DV], F32, A + 32 * KB)
    o_tok = at("o_tok", [P, NT, GH * DV], F32, A + 46 * KB)
    o_sq = at("o_sq", [P, 2, GH * DV], F32, A + 54 * KB)
    decay = at("decay", [P, 2, T // CHUNK], F32, A + 58 * KB)
    kinds = {n: at(n, [P, NT, AH, HD], F32, Y + 6 * KB * i)
             for i, n in enumerate(["aq", "ak", "av", "bq", "bk", "bv", "ag", "bg"])}
    m_flat = at("m_flat", [P, NT, 2 * WE], F32, A)
    mkv_flat = at("mkv_flat", [P, NMEM // P, 2 * WE], F32, A + 8 * KB)
    m_tok = m_flat[:, :, :].rearrange("p t (s h d) -> p t s h d", s=2, h=EH)
    mkv = mkv_flat[:, :, :].rearrange("p t (s h d) -> p t s h d", s=2, h=EH)
    W2 = A + 12 * KB
    mem_x = [at(f"mem_x{l}", [P, NMEM // P, D], F32, A + (16, 38)[l] * KB) for l in range(DEPTH)]
    mem_n = [at(f"mem_n{l}", [P, NMEM // P, D], F32, A + (24, 46)[l] * KB) for l in range(DEPTH)]
    rope_2 = [at(f"rope_2{i}", [P, NT, AH, HD // 2], F32, A + 38 * KB + 3 * KB * i) for i in range(4)]
    sq_2 = at("sq_2", [P, 2, AH, HD], F32, A + 50 * KB)
    table_2 = at("table_2", [P, 4, NT, HD // 2], F32, A + 53 * KB)
    mem_hi = at("mem_hi", [P, KD, NMEM], F32R, Y + 16 * KB)
    mem_lo = at("mem_lo", [P, KD, NMEM], F32R, Y + 24 * KB)
    qT, probs, probsT, masked = [
        [at(f"{n}{i + 1}", [P, 3 if n == "masked" else 2, T], F32, base + offs[i] * KB)
         for i, base in enumerate([W1, W2])]
        for n, offs in (("qT", (0, 0)), ("probs", (8, 12)), ("probsT", (12, 16)), ("masked", (16, 20)))]
    kT_1 = at("kT_1", [P, 2, T], F32, W1 + 4 * KB)
    kT_2 = at("kT_2", [P, 2, 2, T], F32, W2 + 4 * KB)

    def spread(ap):
        return ap.partition_broadcast(P)

    const_loads = [
        (ident[:, :], w["k_ident"]), (mask_chunk[:, :], w["k_mask_chunk"]),
        (mask_causal[:, :], w["k_mask_causal"]), (mask_dilated[:, :], w["k_mask_dilated"]),
        (inv_freq[:, :], w["k_inv"]), (cos2[:, :, :], w["k_cos2"].rearrange("(t p) f -> p t f", p=P)),
        (sin2[:, :, :], w["k_sin2"].rearrange("(t p) f -> p t f", p=P)),
        (pos_rows[R_POS:R_POS + NT, :], w["positions"].rearrange("a (t p) -> (a t) p", p=P)),
    ]

    def rows_at(r, ap):
        n = ap.shape[0] // P
        return vec_rows[r:r + n, :], ap.rearrange("(k p) -> k p", p=P)

    for l in range(DEPTH):
        const_loads += [
            rows_at(R_GATE + 3 * KD * l, w["b_gate"][l]),
            rows_at(R_X + KD * l, w["norm_g"][l]),
            rows_at(R_X + KD * (DEPTH + l), w["norm_g_2"][l]),
            rows_at(R_MEM + KD * l, w["mem_norm_g_2"][l]),
            rows_at(R_C + 3 * l, w["mla_cq_g"][l]),
            rows_at(R_C + 3 * l + 2, w["mla_ckv_g"][l]),
            rows_at(R_GLA + 2 * l, w["gla_b_gate"][l]),
            (w_gu[:, l, :], w["gla_w_gate"][l]),
            (gain_q[:, l, :], spread(w["mla_q_g"][l])), (gain_k[:, l, :], spread(w["mla_k_g"][l])),
            (gain_o[:, l, :], spread(w["gla_o_g"][l])), (gain_2[:, l, :, :], spread(w["qk_g_2"][l])),
        ]

    def vec_col(r, n=1):
        return vec_cols[:, r:r + n]

    N_CONST = len(const_loads)

    gemm_bank = [stack.enter_context(nc.psum_tensor(f"gemm_bank{b}", [P, T], F32)) for b in range(4)]
    aux_bank = [stack.enter_context(nc.psum_tensor(f"aux_bank{b}", [P, T], F32)) for b in range(4)]

    def sem(name):
        return stack.enter_context(nc.semaphore(name))

    consts_loaded = sem("consts_loaded")
    x_loaded = sem("x_loaded")
    mem_loaded = sem("mem_loaded")
    sg_loaded = sem("sg_loaded")
    gla_loaded = sem("gla_loaded")
    raw_loaded = [sem(f"raw_loaded{i}") for i in range(RAW)]
    w_hi_ready = sem("w_hi_ready")
    w_lo_ready = sem("w_lo_ready")
    w_used = sem("w_used")
    gemm_full = [sem(f"gemm_full{b}") for b in range(4)]
    gemm_read = [sem(f"gemm_read{b}") for b in range(4)]
    aux_full = [sem(f"aux_full{b}") for b in range(4)]
    aux_read = [sem(f"aux_read{b}") for b in range(4)]
    scalar_done = sem("scalar_done")
    vector_done = sem("vector_done")
    pool_done = sem("pool_done")
    squares_ready = sem("squares_ready")
    sums_ready = sem("sums_ready")
    rstd_ready = sem("rstd_ready")
    rows_scaled = sem("rows_scaled")
    mem_scaled = sem("mem_scaled")
    head_sq_ready = sem("head_sq_ready")
    head_sq_read = sem("head_sq_read")
    k_rope_ready = sem("k_rope_ready")
    o_sq_ready = sem("o_sq_ready")
    o_sq_read = sem("o_sq_read")
    zc_ready = sem("zc_ready")
    feat_hi_ready = sem("feat_hi_ready")
    positions_ready = sem("positions_ready")
    rope_ready = sem("rope_ready")
    sines_ready = sem("sines_ready")
    c_scaled = sem("c_scaled")
    vn_ready = sem("vn_ready")
    ya_ready = sem("ya_ready")
    ya_hi_ready = sem("ya_hi_ready")
    ya_lo_ready = sem("ya_lo_ready")
    heads_ready = sem("heads_ready")
    rows_gated = sem("rows_gated")
    probs_ready = sem("probs_ready")
    silu_ready = sem("silu_ready")
    gla_gate = sem("gla_gate")
    gla_exp = sem("gla_exp")
    gla_qk = sem("gla_qk")
    pads_zeroed = sem("pads_zeroed")
    keys_zeroed = sem("keys_zeroed")
    gate_ready = sem("gate_ready")
    merged_ready = sem("merged_ready")
    merged_hi_ready = sem("merged_hi_ready")
    merged_lo_ready = sem("merged_lo_ready")
    out_stored = sem("out_stored")

    UNITS_1, UNITS_2 = MH * NT, (AH + BH + EH) * NT

    group_key = {gi: key for key, gi in gindex.items()}

    def gi_of(*key):
        return gindex[key]

    def wait_gemm_full(eng, gi, b):
        eng.wait_ge(gemm_full[b], bank_use[gi, b] + 1)

    def wait_gemm_read(eng, gi, b=None):
        for i in (range(groups[gi].banks) if b is None else [b]):
            eng.wait_ge(gemm_read[i], bank_use[gi, i] + 1)

    def wait_group_done(eng, gi):
        wait_gemm_full(eng, gi, groups[gi].banks - 1)

    def wait_step_used(eng, s):
        gi, kk = step_group[s]
        if kk == groups[gi].K - 1:
            wait_group_done(eng, gi)
        else:
            eng.wait_ge(w_used, steps_marked[s])

    aux_place = {}
    aux_count = [0]

    def aux_open(key):
        n = aux_count[0]
        aux_count[0] += 1
        b, use = n % 4, n // 4
        assert key not in aux_place, key
        aux_place[key] = (b, use)
        if use:
            nc.tensor.wait_ge(aux_read[b], use)
        return aux_bank[b]

    def aux_wait_full(eng, key):
        b, use = aux_place[key]
        eng.wait_ge(aux_full[b], use + 1)
        return aux_bank[b]

    def aux_wait_read(eng, key):
        b, use = aux_place[key]
        eng.wait_ge(aux_read[b], use + 1)

    def full_of(key):
        return aux_full[aux_place[key][0]]

    def read_of(key):
        return aux_read[aux_place[key][0]]

    def flat_2(name):
        return m_flat if name == "m" else kinds[name][:, :, :, :].rearrange("p t h d -> p t (h d)")

    def y2_key(l, kk):
        return [((2, l, "yaq", kk)), (2, l, "ybq", kk - 3), (2, l, "ym", kk - 6)][min(kk // 3, 2)]

    def next_mem(block, l):
        return l + 1 if block == 2 and l + 1 < DEPTH else 0 if block == 1 and l == DEPTH - 1 else None

    block = stack.enter_context(nc.Block())

    BESIDE = {("mla", l): [(1, l, g) for g in ("qkc", "gc", "vc")] for l in range(DEPTH)}
    BESIDE |= {("moba", l): [(2, l, g) for g in ("bv", "m")] for l in range(DEPTH)}
    BESIDE |= {("dilated", l): [(2, l, g) for g in ("ag", "bg")] for l in range(DEPTH)}
    BESIDE |= {("memory", l): [(2, l, "out", 0)] for l in range(DEPTH)}
    TURNS_FIRST = 6

    def beside(name, l, n_units):
        keys = [gindex[g] for g in BESIDE[name, l]]
        steps = [first_step[gi] + kk for gi in keys for kk in range(groups[gi].K)]
        late = 0
        if name == "memory":
            steps, late = steps[:TURNS_FIRST], TURNS_FIRST
        work = [(s, b) for s in steps for b in range(groups[step_group[s][0]].banks)]
        out = []
        for n in range(n_units):
            i, of = max(0, n - late), n_units - late
            part = work[i * len(work) // of:(i + 1) * len(work) // of] if n >= late else []
            ended = []
            for s, b in part:
                gi, kk = step_group[s]
                if kk == groups[gi].K - 1 and b == groups[gi].banks - 1:
                    ended.append(gi)
            out.append((part, ended))
        return out

    class Attention:

        def __init__(self, name, l, heads, group, d, q_of, k_of, v_of, n_keys, mask, out_of, first_unit, where):
            self.name, self.l, self.heads, self.group, self.d = name, l, heads, group, d
            self.q_of, self.k_of, self.v_of, self.out_of = q_of, k_of, v_of, out_of
            self.n_keys, self.mask, self.first_unit, self.where = n_keys, mask, first_unit, where
            self.units = [(h, i) for h in range(heads) for i in range(NT)]
            self.k_tiles = max(n_keys(i) for i in range(NT))
            self.scale = d ** -0.5
            self.rows = d * group

        def turns_next(self, n):
            h, i = self.units[n]
            return h + 1 if i == 1 and (h + 1) % self.group == 0 and h + 1 < self.heads else None

        def qT_of(self, h):
            return qT[self.where][0:self.rows, h // self.group % 2, :]

        def kT_of(self, h):
            return kT_2[:, h // 2 % 2, h % 2, :] if self.group == 2 else kT_1[0:self.rows, h % 2, :]

    def attention_1(l):
        return Attention("mla", l, MH, 1, QK,
                         lambda h, t: q[:, t, h, :], lambda h, t: k[:, t, h, :],
                         lambda h, t: v_mla[:, t, h, :], lambda i: i + 1,
                         lambda i: mask_chunk[:, T - (i + 1) * P:T],
                         lambda h, t: q[:, t, h, 0:MV], l * UNITS_1, 0)

    def attention_2(l, name):
        base = DEPTH * UNITS_1 + l * UNITS_2

        def pair(flat, h, t):
            return flat[:, t, h * HD:(h + 2) * HD]

        if name == "memory":
            return Attention(name, l, EH, 2, HD,
                             lambda h, t: pair(m_flat, h, t), lambda h, t: pair(mkv_flat, h, t),
                             lambda h, t: mkv[:, t, 1, h, :], lambda i: NMEM // P,
                             lambda i: mask_chunk[:, 0:NMEM],
                             lambda h, t: m_tok[:, t, 0, h, :], base + (AH + BH) * NT, 1)
        a = "a" if name == "moba" else "b"
        mask = mask_causal if name == "moba" else mask_dilated
        return Attention(name, l, AH, 2, HD,
                         lambda h, t: pair(flat_2(a + "q"), h, t), lambda h, t: pair(flat_2(a + "k"), h, t),
                         lambda h, t: kinds[a + "v"][:, t, h, :], lambda i: i + 1,
                         lambda i: mask[:, T - (i + 1) * P:T],
                         lambda h, t: kinds[a + "q"][:, t, h, :],
                         base + (0 if name == "moba" else AH * NT), 1)

    @block.tensor
    def _(pe):
        def transposes(key, source, n_k, n_t, rows=P):
            for kk in range(n_k):
                bank = aux_open((*key, kk))
                for t in range(n_t):
                    last = pe.transpose(bank[0:rows, t * P:(t + 1) * P], source(t, kk), ident[:, :])
                last.then_inc(full_of((*key, kk)), 1)

        def step(s, mode, act, ready=None, banks=None):
            gi, kk = step_group[s]
            g = groups[gi]
            slot = s % RING
            hi, lo = act(kk)
            if banks is None or banks[0] == 0:
                if ready:
                    ready(kk)
                pe.wait_ge(w_lo_ready, s + 1)
            for b in (range(g.banks) if banks is None else banks):
                if kk == 0 and bank_use[gi, b]:
                    pe.wait_ge(gemm_read[b], bank_use[gi, b])
                begin, end = kk == 0, kk == g.K - 1
                if mode == "features":
                    m = min(P, g.n)
                    cols = slice(b * P, b * P + m)
                    o = gemm_bank[b][0:m, 0:T]
                    passes = [(w_hi[:, slot, cols], hi), (w_hi[:, slot, cols], lo), (w_lo[:, slot, cols], hi)]
                else:
                    o = gemm_bank[b][:, 0:g.n]
                    tok = slice(b * P, (b + 1) * P)
                    passes = [(hi[:, tok], w_hi[:, slot, 0:g.n]), (hi[:, tok], w_lo[:, slot, 0:g.n]),
                              (lo[:, tok], w_hi[:, slot, 0:g.n])]
                for n, (a, c) in enumerate(passes):
                    last = pe.matmul(o, a, c, start=begin and n == 0, stop=end and n == 2)
                if end:
                    last.then_inc(gemm_full[b], 1)
                elif b == g.banks - 1:
                    last.then_inc(w_used, 1)

        def parts(hi, lo, k0=0):
            return lambda kk: (hi[:, k0 + kk, :], lo[:, k0 + kk, :])

        x_parts = parts(act_hi, act_lo)

        def gemm(gi, mode, act=x_parts, ready=None, ks=None):
            for kk in (range(groups[gi].K) if ks is None else ks):
                step(first_step[gi] + kk, mode, act, ready)

        def normed(key, n_t, count):
            pe.wait_ge(rows_scaled, count)
            source = x_n[key[0] - 1]
            transposes(key, lambda t, kk: source[:, t, kk * P:(kk + 1) * P], KD, n_t)

        def part_ready(key):
            return lambda kk: aux_wait_read(pe, (*key, kk))

        def attention(a, mode_of, ready=None, extra=None):
            side = beside(a.name, a.l, len(a.units))

            def turn(h):
                for what, of, n in (("q", a.q_of, NT), ("k", a.k_of, a.k_tiles)):
                    transposes((a.name, a.l, what, h), lambda t, kk: of(h, t), 1, n, a.rows)

            def filler(work):
                for s, b in work:
                    step(s, mode_of[group_key[step_group[s][0]]], x_parts, ready, [b])

            def scores(n):
                h, i = a.units[n]
                if i == 0 and h % a.group == 0:
                    aux_wait_read(pe, (a.name, a.l, "q", h, 0))
                    aux_wait_read(pe, (a.name, a.l, "k", h, 0))
                key = (a.name, a.l, "S", n)
                bank = aux_open(key)
                pe.matmul(bank[:, 0:a.n_keys(i) * P], a.qT_of(h)[:, i * P:(i + 1) * P],
                          a.kT_of(h)[:, 0:a.n_keys(i) * P],
                          start=True, stop=True).then_inc(full_of(key), 1)

            def turn_probs(n):
                h, i = a.units[n]
                pe.wait_ge(probs_ready, a.first_unit + n + 1)
                key = (a.name, a.l, "T", n)
                bank = aux_open(key)
                for j in range(a.n_keys(i)):
                    last = pe.transpose(bank[:, j * P:(j + 1) * P], probs[a.where][:, n % 2, j * P:(j + 1) * P],
                                        ident[:, :])
                last.then_inc(full_of(key), 1)

            def values(n):
                h, i = a.units[n]
                aux_wait_read(pe, (a.name, a.l, "T", n))
                key = (a.name, a.l, "O", n)
                bank = aux_open(key)
                for j in range(a.n_keys(i)):
                    last = pe.matmul(bank[:, 0:HD], probsT[a.where][:, n % 2, j * P:(j + 1) * P], a.v_of(h, j),
                                     start=(j == 0), stop=(j == a.n_keys(i) - 1))
                last.then_inc(full_of(key), 1)

            turn(0)
            filler(side[0][0])
            if extra:
                extra(0)
            scores(0)
            scores(1)
            for n, (h, i) in enumerate(a.units):
                if a.turns_next(n) is not None:
                    turn(a.turns_next(n))
                if n + 2 < len(a.units):
                    scores(n + 2)
                if n:
                    filler(side[n][0])
                if extra and n:
                    extra(n)
                if n:
                    values(n - 1)
                turn_probs(n)
            values(len(a.units) - 1)

        def block_1(l):
            normed((1, l, "x"), NT, l * NT + NT)
            gemm(gi_of(1, l, "c"), "tokens", ready=part_ready((1, l, "x")))
            gemm(gi_of(1, l, "v"), "tokens")
            pe.wait_ge(c_scaled, l + 1)
            transposes((1, l, "c"), lambda t, kk: c_tok[:, t, kk * P:(kk + 1) * P], 3, NT)
            for i in range(2):
                gemm(gi_of(1, l, "uq", i), "tokens", parts(c_hi, c_lo), part_ready((1, l, "c")))
            for i in range(2):
                gemm(gi_of(1, l, "ukv", i), "tokens", parts(c_hi, c_lo, 2),
                     lambda kk: aux_wait_read(pe, (1, l, "c", 2)))
            pe.wait_ge(sg_loaded, 64 * (l + 1))
            transposes((1, l, "sgw"), lambda t, kk: sg_w_raw[:, t, :], 1, 4)
            gemm(gi_of(1, l, "u"), "features")
            gemm(gi_of(1, l, "za"), "features")
            gemm(gi_of(1, l, "zb"), "tokens")
            pe.wait_ge(vn_ready, l + 1)
            aux_wait_read(pe, (1, l, "sgw", 0))
            for g in range(4):
                key = (1, l, "sv", g)
                bank = aux_open(key)
                for n in range(NT):
                    last = pe.matmul(bank[:, n * P:(n + 1) * P], vn[:, n, g * P:(g + 1) * P], sg_wT[:, g, :],
                                     start=True, stop=True)
                last.then_inc(full_of(key), 1)
            pe.wait_ge(heads_ready, l + 1)
            attention(attention_1(l), {(1, l, "qkc"): "features", (1, l, "gc"): "features",
                                       (1, l, "vc"): "tokens"})
            wait_gemm_read(pe, gi_of(1, l, "gc"))
            for m in range(2):
                key = (1, l, "gl", m)
                bank = aux_open(key)
                pe.matmul(bank[:, :], w_gu[:, l, m * P:(m + 1) * P], g_T[:, :],
                          start=True, stop=True).then_inc(full_of(key), 1)
            pe.wait_ge(rows_gated, NT * (2 * l + 1))
            transposes((1, l, "yb"), lambda t, kk: yb_tok[:, t, kk * P:(kk + 1) * P], 4, NT)
            gemm(gi_of(1, l, "zc"), "tokens")
            gla(l)

            def merge(j, i):
                gemm(gi_of(1, l, ("gate", j, i)), "features")
                if i == 0:
                    ready = lambda kk: pe.wait_ge(ya_lo_ready, 4 * (l + 1))
                else:
                    ready = part_ready((1, l, "yb" if i == 1 else "yc"))
                gemm(gi_of(1, l, "branch", j, i), "features", parts(y_hi[i], y_lo[i]), ready)

            merge(0, 0)
            merge(0, 1)
            pe.wait_ge(rows_gated, NT * (2 * l + 2))
            transposes((1, l, "yc"), lambda t, kk: o_tok[:, t, kk * P:(kk + 1) * P], 4, NT)
            merge(0, 2)
            for i in range(3):
                merge(1, i)
            tail(1, l, lambda kk: (merged_hi[kk // 4][:, kk % 4, :], merged_lo[kk // 4][:, kk % 4, :]),
                 lambda kk: pe.wait_ge(merged_lo_ready, KD * l + kk + 1))

        def tail(block, l, act, ready, done=0):
            gemm(gi_of(block, l, "out", 0), "tokens", act, ready, range(done, KD))
            last_out = gi_of(block, l, "out", 1)
            gemm(last_out, "tokens", act, ready, range(0, 4))
            nxt = next_mem(block, l)
            if nxt is not None:
                pe.wait_ge(mem_scaled, (NMEM // P) * (nxt + 1))
                transposes((2, nxt, "mem"), lambda t, kk: mem_n[nxt][:, t, kk * P:(kk + 1) * P], KD, NMEM // P)
            gemm(last_out, "tokens", act, ready, range(4, KD))
            if nxt is not None:
                gemm(gi_of(2, nxt, "mkv"), "tokens", parts(mem_hi, mem_lo), part_ready((2, nxt, "mem")))

        def gla(l):
            pe.wait_ge(gla_qk, 2 * l + 2)
            transposes((1, l, "ks"), lambda t, kk: qk_c[:, 2 + kk, t * P:(t + 1) * P], 2, NT)
            wait_gemm_read(pe, gi_of(1, l, "vc"))
            for h in range(GH):
                key = (1, l, "att", h)
                bank = aux_open(key)
                for t in range(NT):
                    last = pe.matmul(bank[:, t * P:(t + 1) * P], kt_pad[:, h // 2, h % 2, t * P:(t + 1) * P],
                                     qk_c[:, h // 2, t * P:(t + 1) * P], start=True, stop=True)
                last.then_inc(full_of(key), 1)
            for m in range(2):
                aux_wait_read(pe, (1, l, "ks", m))
            for n in range(T // CHUNK - 1):
                key = (1, l, "U", n)
                bank = aux_open(key)
                half = slice(CHUNK * (n % 2), CHUNK * (n % 2) + CHUNK)
                for m in range(2):
                    last = pe.matmul(bank[:, m * 2 * DV:(m + 1) * 2 * DV], ks_tok[half, n // 2, m * P:(m + 1) * P],
                                     vc[half, n // 2, m * 2 * DV:(m + 1) * 2 * DV], start=True, stop=True)
                last.then_inc(full_of(key), 1)
            for t in range(NT):
                key = (1, l, "o", t)
                bank = aux_open(key)
                if t == 0:
                    for h in range(GH):
                        aux_wait_read(pe, (1, l, "att", h))
                for h in range(GH):
                    pe.matmul(bank[:, h * DV:(h + 1) * DV], att[:, h, t, :], vc[:, t, h * DV:(h + 1) * DV],
                              start=(h == 0), stop=False, skip_group_check=True)
                for par in range(2):
                    n = 2 * t + par
                    if n == 0:
                        continue
                    aux_wait_read(pe, (1, l, "U", n - 1))
                    for m in range(2):
                        last = pe.matmul(bank[par * CHUNK:(par + 1) * CHUNK, m * 2 * DV:(m + 1) * 2 * DV],
                                         qk_c[:, m, n * CHUNK:(n + 1) * CHUNK], state[:, n - 1, m, :],
                                         start=False, stop=(par == 1 and m == 1), skip_group_check=True)
                last.then_inc(full_of(key), 1)

        def block_2(l):
            normed((2, l, "x"), NT, NT * DEPTH + NT * (l + 1))
            gemm(gi_of(2, l, "aq"), "tokens", ready=part_ready((2, l, "x")))
            for name in ("ak", "av", "bq", "bk"):
                gemm(gi_of(2, l, name), "tokens")
            modes = {(2, l, g): "tokens" for g in ("bv", "m", "ag", "bg")}
            modes[2, l, "out", 0] = "tokens"
            wait_gemm_read(pe, gi_of(2, l, "av"))
            pe.wait_ge(heads_ready, DEPTH + 3 * l + 1)
            attention(attention_2(l, "moba"), modes)
            wait_gemm_read(pe, gi_of(2, l, "bv"))
            pe.wait_ge(heads_ready, DEPTH + 3 * l + 2)
            attention(attention_2(l, "dilated"), modes)
            pe.wait_ge(heads_ready, DEPTH + 3 * l + 3)

            def turn_y(n):
                if n < 2 * 3:
                    name, kk = ("aq", n) if n < 3 else ("bq", n - 3)
                    pe.wait_ge(rows_gated, 2 * NT * DEPTH + NT * (3 * l + 1 + n // 3))
                    bank = aux_open((2, l, "y" + name, kk))
                    for t in range(NT):
                        last = pe.transpose(bank[:, t * P:(t + 1) * P], flat_2(name)[:, t, kk * P:(kk + 1) * P],
                                            ident[:, :])
                    last.then_inc(full_of((2, l, "y" + name, kk)), 1)

            y_ready = lambda kk: aux_wait_read(pe, y2_key(l, kk))
            attention(attention_2(l, "memory"), modes, y_ready, turn_y)
            pe.wait_ge(rows_gated, 2 * NT * DEPTH + NT * (3 * l + 3))
            transposes((2, l, "ym"), lambda t, kk: m_flat[:, t, kk * P:(kk + 1) * P], 2, NT)
            tail(2, l, x_parts, y_ready, TURNS_FIRST)

        pe.wait_ge(consts_loaded, 16 * N_CONST)
        pe.wait_ge(positions_ready, 1)
        bank = aux_open("vec")
        pe.transpose(bank[:, 0:N_ROWS], vec_rows[0:N_ROWS, :], ident[0:N_ROWS, 0:N_ROWS]).then_inc(full_of("vec"), 1)
        for l in range(DEPTH):
            block_1(l)
        for l in range(DEPTH):
            block_2(l)



    class Splitter:

        def __init__(self, do):
            self.at, self.do = 0, do

        def through(self, gi):
            self.to(first_step[gi] + groups[gi].K + AHEAD)

        def beside(self, gi, kk):
            self.to(first_step[gi] + kk + 1 + AHEAD)

        def to(self, s):
            while self.at < min(s, len(step_group)):
                self.do(self.at)
                self.at += 1

    def split_beside(split, side, n, evict_beside):
        for gi in side[n][1]:
            split.to(first_step[gi] + groups[gi].K)
            if evict_beside:
                evict_beside(gi)
        done = [s for part, _ in side[:n + 1] for s, _ in part]
        if done:
            split.to(done[-1] + 1 + AHEAD)

    @block.scalar
    def _(act):
        marks = [0]

        def mark(ins):
            ins.then_inc(scalar_done, 1)
            marks[0] += 1

        def settle():
            act.wait_ge(scalar_done, marks[0])

        def round_weights(s):
            gi, kk = step_group[s]
            p = first_piece[gi] + kk // PIECE
            n = groups[gi].n
            act.wait_ge(raw_loaded[p % RAW], 16 * (p // RAW + 1))
            if s >= RING:
                wait_step_used(act, s - RING)
            act.activation(w_hi[:, s % RING, 0:n], raw[:, p % RAW, kk % PIECE, 0:n], ACT.Copy)\
               .then_inc(w_hi_ready, 1)

        split = Splitter(round_weights)

        def squares_x(j):
            for t in range(NT):
                act.activation(squared[:, j, t, :], x[:, t, j * T:(j + 1) * T], ACT.Square, scale=D ** -0.5,
                               accum_out=sums[:, j * NT + t:j * NT + t + 1]).then_inc(squares_ready, 1)

        head_tiles = [0]

        def head_squares(tiles, sq):
            for tile in tiles:
                n = head_tiles[0]
                head_tiles[0] += 1
                if n >= 2:
                    act.wait_ge(head_sq_read, n - 1)
                heads, d = tile.shape[1], tile.shape[2]
                act.activation(sq[:, n % 2, 0:heads, 0:d], tile, ACT.Square).then_inc(head_sq_ready, 1)
                yield

        def features(key, n_k, n_cols, hi, gain=None, k0=0):
            for kk in range(n_k):
                bank = aux_wait_full(act, (*key, kk))
                scale = 1.0 if gain is None else gain[:, kk:kk + 1]
                act.activation(hi[:, k0 + kk, :], bank[:, 0:n_cols], ACT.Copy, scale=scale)\
                   .then_inc(feat_hi_ready, 1)

        def evict(gi, func, dst):
            split.through(gi)
            evict_now(gi, func, dst)

        def evict_now(gi, func, dst):
            for b in range(groups[gi].banks):
                wait_gemm_full(act, gi, b)
                act.activation(dst(b), gemm_bank[b][:, 0:groups[gi].n], func).then_inc(gemm_read[b], 1)

        def attention(a, evict_beside=None, extra=None, extra_first=False):
            side = beside(a.name, a.l, len(a.units))

            def exponentials(n):
                h, i = a.units[n]
                g = a.first_unit + n
                c = g % 64
                keys = a.n_keys(i) * P
                aux_wait_read(act, (a.name, a.l, "S", n))
                if n >= 2:
                    aux_wait_full(act, (a.name, a.l, "T", n - 2))
                act.activation(probs[a.where][:, n % 2, 0:keys], masked[a.where][:, n % 3, 0:keys], ACT.Exp,
                               bias=neg_max[:, c:c + 1], scale=-1.0, accum_out=row_sum[:, c:c + 1])\
                   .then_inc(probs_ready, 1)

            def turned(n):
                h, i = a.units[n]
                keys = a.n_keys(i) * P
                bank = aux_wait_full(act, (a.name, a.l, "T", n))
                if n >= 2:
                    aux_wait_full(act, (a.name, a.l, "O", n - 2))
                act.activation(probsT[a.where][:, n % 2, 0:keys], bank[:, 0:keys], ACT.Copy)\
                   .then_inc(read_of((a.name, a.l, "T", n)), 1)

            if extra_first:
                extra(0)
            exponentials(0)
            for n in range(len(a.units)):
                if n + 1 < len(a.units):
                    exponentials(n + 1)
                split_beside(split, side, n, evict_beside)
                turned(n)
                if extra and not (extra_first and n == 0):
                    extra(n)

        def block_1(l):
            if l:
                wait_group_done(act, gi_of(1, l - 1, "out", 1))
            act.dma_start(sg_w_raw[:, :, :], w["sg_w"][l].rearrange("g i j -> i g j")).then_inc(sg_loaded, 16)
            act.dma_start(sg_bias[:, :, :], spread(w["sg_b"][l])).then_inc(sg_loaded, 16)
            act.dma_start(ln_g[:, :], spread(w["sg_ln_g"][l])).then_inc(sg_loaded, 16)
            act.dma_start(ln_b[:, :], spread(w["sg_ln_b"][l])).then_inc(sg_loaded, 16)
            if l == 0:
                split.to(RING)
                aux_wait_read(act, "vec")
            features((1, l, "x"), KD, T, act_hi, vec_col(R_X + KD * l, KD))
            if l == 0:
                act.wait_ge(rope_ready, 1)
                act.activation(sin1[:, :, :], angle[:, 0, :, :], ACT.Sin).then_inc(sines_ready, 1)
                act.activation(cos1[:, :, :], angle[:, 1, :, :], ACT.Sin).then_inc(sines_ready, 1)
            evict(gi_of(1, l, "c"), ACT.Copy, lambda b: c_tok[:, b, :])
            evict(gi_of(1, l, "v"), ACT.Gelu_apprx_tanh, lambda b: vn[:, b, :])
            features((1, l, "c"), 3, T, c_hi, vec_col(R_C + 3 * l, 3))
            evict(gi_of(1, l, "uq", 0), ACT.Copy, lambda b: q[:, b, 0:4, :])
            split.through(gi_of(1, l, "uq", 1))
            gi = gi_of(1, l, "ukv", 0)
            split.through(gi)
            for b in range(NT):
                wait_gemm_full(act, gi, b)
                kv = gemm_bank[b][:, :].rearrange("p (h c) -> p h c", h=4)
                act.activation(k[:, b, 0:4, 0:NOPE], kv[:, :, 0:NOPE], ACT.Copy)
                act.activation(v_mla[:, b, 0:4, :], kv[:, :, NOPE:NOPE + MV], ACT.Copy).then_inc(gemm_read[b], 1)
            split.through(gi_of(1, l, "ukv", 1))
            wait_gemm_read(act, gi_of(1, l, "uq", 0))
            wait_gemm_read(act, gi_of(1, l, "uq", 1))
            wait_group_done(act, gi_of(1, l, "ukv", 1))
            split.beside(gi_of(1, l, "u"), 2)
            for t, _ in enumerate(head_squares([q[:, t, :, :] for t in range(NT)], sq_1)):
                split.beside(gi_of(1, l, "u"), 3 + t // 2)
            wait_gemm_read(act, gi_of(1, l, "ukv", 0))
            wait_gemm_read(act, gi_of(1, l, "ukv", 1))
            act.wait_ge(k_rope_ready, NT * (l + 1))
            for t, _ in enumerate(head_squares([k[:, t, :, :] for t in range(NT)], sq_1)):
                split.beside(gi_of(1, l, "u"), 5 + t // 2)
            evict(gi_of(1, l, "u"), ACT.Gelu_apprx_tanh, lambda b: u[:, b, :])
            evict(gi_of(1, l, "za"), ACT.Silu, lambda b: za[:, b, :])
            evict(gi_of(1, l, "zb"), ACT.Silu, lambda b: zb[:, b, :])
            for g in range(4):
                act.wait_ge(ya_ready, 4 * l + g + 1)
                act.activation(y_hi[0][:, g, :], u[:, g, :], ACT.Copy).then_inc(ya_hi_ready, 1)
            attention(attention_1(l))
            aux_wait_full(act, ("mla", l, "k", MH - 1, 0))
            act.dma_start(keep[:, :, :], w["k_keep"].rearrange("p (t i) -> p t i", t=NT)).then_inc(gla_loaded, 16)
            act.dma_start(carry[:, :], w["k_carry"]).then_inc(gla_loaded, 16)
            g_zc = gi_of(1, l, "zc")
            split.beside(g_zc, 0)
            features((1, l, "yb"), 4, T, y_hi[1])
            split.beside(g_zc, 1)
            act.wait_ge(gla_gate, 3 * l + 1)
            mark(act.activation(log_t[:, :, :], log_t[:, :, :], ACT.Exp))
            split.beside(g_zc, 2)
            settle()
            act.activation(log_t[:, :, :], log_t[:, :, :], ACT.Ln, bias=1.0).then_inc(gla_exp, 1)
            split.beside(g_zc, 4)
            act.wait_ge(gla_gate, 3 * l + 2)
            act.activation(e_up[:, :, :], b_cum[:, :, :], ACT.Exp, scale=1.0 / TAU).then_inc(gla_exp, 1)
            split.beside(g_zc, 5)
            act.activation(e_dn[:, :, :], b_cum[:, :, :], ACT.Exp, scale=-1.0 / TAU).then_inc(gla_exp, 1)
            split.beside(g_zc, 6)
            act.wait_ge(gla_gate, 3 * l + 3)
            act.activation(e_st[:, :, :], e_st[:, :, :], ACT.Exp, scale=1.0 / TAU).then_inc(gla_exp, 1)
            evict(g_zc, ACT.Silu, lambda b: zc[:, b, :])
            for t in range(NT):
                split.beside(gi_of(1, l, ("gate", 0, 0)), t + 1)
                bank = aux_wait_full(act, (1, l, "o", t))
                n = NT * l + t
                if n >= 2:
                    act.wait_ge(o_sq_read, n - 1)
                act.activation(o_tok[:, t, :], bank[:, :], ACT.Copy)
                act.activation(o_sq[:, t % 2, :], bank[:, :], ACT.Square).then_inc(read_of((1, l, "o", t)), 1)

            def merge(j, i):
                n = 3 * j + i
                gi = gi_of(1, l, ("gate", j, i))
                split.through(gi)
                for m in range(4):
                    wait_gemm_full(act, gi, m)
                    if n >= 2:
                        wait_gemm_read(act, gi_of(1, l, "branch", (n - 2) // 3, (n - 2) % 3), m)
                    c = i * KD + j * 4 + m
                    act.activation(gate[:, n % 2, m, :], gemm_bank[m][:, :], ACT.Sigmoid,
                                   bias=vec_col(R_GATE + 3 * KD * l + c)).then_inc(gemm_read[m], 1)
                split.through(gi_of(1, l, "branch", j, i))

            def split_merged(j):
                for m in range(4):
                    act.wait_ge(merged_ready, KD * l + 4 * j + m + 1)
                    act.activation(merged_hi[j][:, m, :], merged[:, 4 * j + m, :], ACT.Copy)\
                       .then_inc(merged_hi_ready, 1)

            merge(0, 0)
            merge(0, 1)
            features((1, l, "yc"), 4, T, y_hi[2])
            merge(0, 2)
            merge(1, 0)
            split_merged(0)
            merge(1, 1)
            merge(1, 2)
            split_merged(1)
            wait_gemm_read(act, gi_of(1, l, "branch", 1, 2))
            tail(1, l)

        def tail(block, l):
            nxt = next_mem(block, l)
            if nxt is not None:
                act.dma_start(mem_x[nxt][:, :, :], w["mem_2"][0].rearrange("(t p) d -> p t d", p=P))\
                   .then_inc(mem_loaded, 16)
            split.through(gi_of(block, l, "out", 0))
            if nxt is not None:
                act.wait_ge(mem_loaded, 16 * (nxt + 1))
                for t in range(NMEM // P):
                    act.activation(mem_n[nxt][:, t, :], mem_x[nxt][:, t, :], ACT.Square, scale=D ** -0.5,
                                   accum_out=sums[:, 64 + t:65 + t]).then_inc(squares_ready, 1)
            last = block == 2 and l == DEPTH - 1
            if not last:
                wait_gemm_read(act, gi_of(block, l, "out", 0))
                squares_x(0)
            split.beside(gi_of(block, l, "out", 1), 3)
            if nxt is not None:
                features((2, nxt, "mem"), KD, NMEM, mem_hi, vec_col(R_MEM + KD * nxt, KD))
            split.through(gi_of(block, l, "out", 1))
            if not last:
                wait_gemm_read(act, gi_of(block, l, "out", 1))
                squares_x(1)
            if nxt is not None:
                evict(gi_of(2, nxt, "mkv"), ACT.Copy, lambda b: mkv_flat[:, b, :])

        def block_2(l):
            features((2, l, "x"), KD, T, act_hi, vec_col(R_X + KD * (DEPTH + l), KD))
            evict(gi_of(2, l, "aq"), ACT.Copy, lambda b: flat_2("aq")[:, b, :])
            split.through(gi_of(2, l, "ak"))

            def kind_tiles(a):
                return [kinds[a + n][:, t, :, :] for n in ("q", "k") for t in range(NT)]

            wait_gemm_read(act, gi_of(2, l, "aq"))
            wait_gemm_read(act, gi_of(2, l, "ak"))
            for n, _ in enumerate(head_squares(kind_tiles("a"), sq_2)):
                split.beside(gi_of(2, l, "av"), n // 2)
            evict(gi_of(2, l, "av"), ACT.Copy, lambda b: flat_2("av")[:, b, :])
            split.through(gi_of(2, l, "bq"))
            evict(gi_of(2, l, "bk"), ACT.Copy, lambda b: flat_2("bk")[:, b, :])
            wait_gemm_read(act, gi_of(2, l, "bq"))
            wait_gemm_read(act, gi_of(2, l, "bk"))
            b_squares = head_squares(kind_tiles("b"), sq_2)

            def twice(work):
                return lambda n: [next(work, None), next(work, None)]

            attention(attention_2(l, "moba"), None, twice(b_squares))
            wait_gemm_read(act, gi_of(2, l, "m"))
            m_squares = head_squares([m_tok[:, t, 0, :, :] for t in range(NT)]
                                     + [mkv[:, t, 0, :, :] for t in range(NMEM // P)], sq_2)

            def evict_gates(gi):
                evict_now(gi, ACT.Silu, lambda b: flat_2(group_key[gi][2])[:, b, :])

            attention(attention_2(l, "dilated"), evict_gates, twice(m_squares))
            act.activation(m_flat[:, :, WE:2 * WE], m_flat[:, :, WE:2 * WE], ACT.Silu).then_inc(silu_ready, 1)

            def y_features(n):
                if n == 0:
                    wait_group_done(act, gi_of(2, l, "bg"))
                if n < TURNS_FIRST:
                    name, kk = ("aq", n) if n < 3 else ("bq", n - 3)
                    bank = aux_wait_full(act, (2, l, "y" + name, kk))
                    act.activation(act_hi[:, n, :], bank[:, :], ACT.Copy).then_inc(feat_hi_ready, 1)

            attention(attention_2(l, "memory"), None, y_features, True)
            features((2, l, "ym"), 2, T, act_hi, None, 6)
            tail(2, l)

        act.wait_ge(x_loaded, 16)
        squares_x(0)
        squares_x(1)
        for l in range(DEPTH):
            block_1(l)
        for l in range(DEPTH):
            block_2(l)

    @block.vector
    def _(dve):
        marks = [0]
        hi_count = [0]

        def mark(ins):
            ins.then_inc(vector_done, 1)
            marks[0] += 1

        def settle():
            dve.wait_ge(vector_done, marks[0])

        def residue(s):
            gi, kk = step_group[s]
            p = first_piece[gi] + kk // PIECE
            n = groups[gi].n
            dve.wait_ge(w_hi_ready, s + 1)
            dve.tensor_tensor(w_lo[:, s % RING, 0:n], raw[:, p % RAW, kk % PIECE, 0:n],
                              w_hi[:, s % RING, 0:n].bitcast(F32), ALU.subtract).then_inc(w_lo_ready, 1)

        split = Splitter(residue)

        def scale_rows(source, dst, n_t, job, s0, done):
            dve.wait_ge(rstd_ready, job)
            for t in range(n_t):
                dve.tensor_scalar(dst[:, t, :], source[:, t, :], rstd[:, s0 + t:s0 + t + 1], None, ALU.mult)\
                   .then_inc(done, 1)

        def features(key, n_k, n_cols, hi, lo, gain=None, k0=0):
            for kk in range(n_k):
                hi_count[0] += 1
                dve.wait_ge(feat_hi_ready, hi_count[0])
                bank = aux_bank[aux_place[(*key, kk)][0]]
                h = hi[:, k0 + kk, :].bitcast(F32)
                if gain is None:
                    ins = dve.tensor_tensor(lo[:, k0 + kk, :], bank[:, 0:n_cols], h, ALU.subtract)
                else:
                    ins = dve.scalar_tensor_tensor(out=lo[:, k0 + kk, :], in0=bank[:, 0:n_cols],
                                                   scalar=gain[:, kk:kk + 1], in1=h,
                                                   op0=ALU.mult, op1=ALU.subtract)
                ins.then_inc(read_of((*key, kk)), 1)

        def evict(gi, dst):
            split.through(gi)
            evict_now(gi, dst)

        def evict_now(gi, dst, rows=P):
            for b in range(groups[gi].banks):
                wait_gemm_full(dve, gi, b)
                dve.tensor_copy(dst(b), gemm_bank[b][0:rows, 0:groups[gi].n]).then_inc(gemm_read[b], 1)

        head_tiles = [0]

        def head_norm(tiles):
            c = 0
            for tile in tiles:
                n, heads, d = head_tiles[0], tile.shape[1], tile.shape[2]
                head_tiles[0] += 1
                dve.wait_ge(head_sq_ready, n + 1)
                sq = sq_1 if d == QK else sq_2
                dve.tensor_reduce(head_sums[:, c:c + heads], sq[:, n % 2, 0:heads, 0:d], AX_X, ALU.add)\
                   .then_inc(head_sq_read, 1)
                c += heads
                yield
            dve.wait_ge(head_sq_read, head_tiles[0])
            yield from inverse_roots(c, 1.0 / d)
            settle()
            c = 0
            for tile in tiles:
                heads, d = tile.shape[1], tile.shape[2]
                r = head_rstd[:, c:c + heads].unsqueeze(2).to_broadcast([P, heads, d])
                mark(dve.tensor_tensor(tile, tile, r, ALU.mult))
                c += heads
                yield

        def inverse_roots(n, scale):
            m, y, z = head_sums[:, 0:n], head_rstd[:, 0:n], newton[:, 0:n]
            mark(dve.tensor_scalar(m, m, scale, EPS, ALU.mult, ALU.add))
            settle()
            mark(dve.tensor_scalar(y.bitcast(I32), m.bitcast(I32), 1, None, ALU.logical_shift_right))
            settle()
            mark(dve.tensor_scalar(y.bitcast(I32), y.bitcast(I32), -1, 0x5f3759df, ALU.mult, ALU.add))
            for _ in range(3):
                settle()
                mark(dve.tensor_tensor(z, y, y, ALU.mult))
                settle()
                mark(dve.scalar_tensor_tensor(out=z, in0=z, scalar=-0.5, in1=m, op0=ALU.mult, op1=ALU.mult))
                settle()
                mark(dve.scalar_tensor_tensor(out=y, in0=z, scalar=1.5, in1=y, op0=ALU.add, op1=ALU.mult))
            yield

        def rotate(tile, d0, half, gain, cos, sin, table, tmp):
            heads = tile.shape[2]
            x1, x2 = tile[:, :, :, d0:d0 + half], tile[:, :, :, d0 + half:d0 + 2 * half]
            g1 = gain[:, d0:d0 + half].unsqueeze(1).to_broadcast([P, NT, half])
            g2 = gain[:, d0 + half:d0 + 2 * half].unsqueeze(1).to_broadcast([P, NT, half])
            settle()
            for i, (trig, g) in enumerate(((cos, g1), (sin, g2), (sin, g1), (cos, g2))):
                mark(dve.tensor_tensor(table[:, i, :, :], trig, g, ALU.mult))
            settle()
            yield
            for i, xx in enumerate((x1, x2, x1, x2)):
                t4 = table[:, i, :, :].unsqueeze(2).to_broadcast([P, NT, heads, half])
                mark(dve.tensor_tensor(tmp[i][:, :, :, :], xx, t4, ALU.mult))
                if i % 2:
                    yield
            settle()
            mark(dve.tensor_tensor(x1, tmp[0][:, :, :, :], tmp[1][:, :, :, :], ALU.subtract))
            mark(dve.tensor_tensor(x2, tmp[2][:, :, :, :], tmp[3][:, :, :, :], ALU.add))
            yield

        def heads_done():
            settle()
            dve.engine_nop().then_inc(heads_ready, 1)

        def alongside(work, gis, per_step, at_end=None):
            for gi in gis:
                for kk in range(groups[gi].K):
                    split.beside(gi, kk)
                    for _ in range(per_step):
                        next(work, None)
                if at_end:
                    at_end(gi)
            for _ in work:
                pass

        def attention(a, evict_beside=None, extra=None, extra_first=False):
            side = beside(a.name, a.l, len(a.units))

            def turned(h):
                key = (a.name, a.l, "q", h, 0)
                bank = aux_wait_full(dve, key)
                dve.tensor_copy(a.qT_of(h), bank[0:a.rows, :]).then_inc(read_of(key), 1)
                key = (a.name, a.l, "k", h, 0)
                bank = aux_wait_full(dve, key)
                for hh in range(a.group):
                    r = slice(hh * a.d, (hh + 1) * a.d)
                    ins = dve.tensor_copy(a.kT_of(h + hh)[r, 0:a.k_tiles * P], bank[r, 0:a.k_tiles * P])
                    if hh == a.group - 1:
                        ins.then_inc(read_of(key), 1)
                    else:
                        mark(ins)

            def scores(n):
                h, i = a.units[n]
                keys = a.n_keys(i) * P
                c = (a.first_unit + n) % 64
                key = (a.name, a.l, "S", n)
                bank = aux_wait_full(dve, key)
                if n >= 3:
                    dve.wait_ge(probs_ready, a.first_unit + n - 2)
                dve.tensor_tensor_reduce(out=masked[a.where][:, n % 3, 0:keys], in0=bank[:, 0:keys], in1=a.mask(i),
                                         scale=-a.scale, scalar=3.0e38, op0=ALU.add, op1=ALU.min,
                                         accum_out=neg_max[:, c:c + 1]).then_inc(read_of(key), 1)

            def values(n):
                h, i = a.units[n]
                c = (a.first_unit + n) % 64
                dve.wait_ge(probs_ready, a.first_unit + n + 1)
                mark(dve.reciprocal(row_inv[:, c:c + 1], row_sum[:, c:c + 1]))
                key = (a.name, a.l, "O", n)
                bank = aux_wait_full(dve, key)
                settle()
                dve.tensor_scalar(a.out_of(h, i), bank[:, 0:HD], row_inv[:, c:c + 1], None, ALU.mult)\
                   .then_inc(read_of(key), 1)

            turned(0)
            if extra_first:
                extra(0)
            scores(0)
            scores(1)
            for n, (h, i) in enumerate(a.units):
                if a.turns_next(n) is not None:
                    turned(a.turns_next(n))
                if n + 2 < len(a.units):
                    scores(n + 2)
                split_beside(split, side, n, evict_beside)
                if extra and not (extra_first and n == 0):
                    extra(n)
                if n:
                    values(n - 1)
            values(len(a.units) - 1)
            aux_wait_read(dve, (a.name, a.l, "O", len(a.units) - 1))

        def update_x(block, l, j):
            gi = gi_of(block, l, "out", j)
            split.through(gi)
            for t in range(NT):
                wait_gemm_full(dve, gi, t)
                xs = x[:, t, j * T:(j + 1) * T]
                dve.tensor_tensor(xs, gemm_bank[t][:, :], xs, ALU.add).then_inc(gemm_read[t], 1)

        def rope_angles():
            flat = [angle[:, i, :, :].rearrange("p t f -> p (t f)") for i in range(4)]
            for t in range(NT):
                mark(dve.tensor_scalar(angle[:, 0, t, :], inv_freq[:, :], vec_col(R_POS + t), None, ALU.mult))
            settle()
            mark(dve.tensor_scalar(flat[1], flat[0], 1.0 / TWO_PI, ROUND, ALU.mult, ALU.add))
            settle()
            mark(dve.tensor_scalar(flat[1], flat[1], ROUND, None, ALU.subtract))
            for part in (PI_1, PI_2, PI_3):
                settle()
                mark(dve.scalar_tensor_tensor(out=flat[0], in0=flat[1], scalar=-part, in1=flat[0],
                                              op0=ALU.mult, op1=ALU.add))
            settle()
            mark(dve.tensor_scalar(flat[0], flat[0], math.pi * (1 - 2 ** -23), -math.pi * (1 - 2 ** -23),
                                   ALU.min, ALU.max))
            settle()
            mark(dve.tensor_scalar(flat[1], flat[0], math.pi / 2, None, ALU.add))
            settle()
            mark(dve.tensor_scalar(flat[2], flat[1], math.pi, -TWO_PI, ALU.is_gt, ALU.mult))
            settle()
            mark(dve.tensor_tensor(flat[1], flat[1], flat[2], ALU.add))
            settle()
            dve.tensor_scalar(flat[1], flat[1], math.pi * (1 - 2 ** -23), -math.pi * (1 - 2 ** -23),
                              ALU.min, ALU.max).then_inc(rope_ready, 1)

        def block_1(l):
            job = 4 * l
            scale_rows(x, x_n[0], NT, job + 1, 0, rows_scaled)
            if l == 0:
                rope_angles()
                split.to(RING)
            features((1, l, "x"), KD, T, act_hi, act_lo, vec_col(R_X + KD * l, KD))
            split.through(gi_of(1, l, "c"))
            wait_gemm_read(dve, gi_of(1, l, "c"))
            split.beside(gi_of(1, l, "v"), 2)
            for t in range(NT):
                for n, (a, b) in enumerate(((0, QR), (QR, QR + KVR))):
                    settle()
                    ins = dve.tensor_tensor_reduce(out=c_sq[:, a:b], in0=c_tok[:, t, a:b], in1=c_tok[:, t, a:b],
                                                   scale=1.0 / (b - a), scalar=0.0, op0=ALU.mult, op1=ALU.add,
                                                   accum_out=sums[:, 8 + n * NT + t:9 + n * NT + t])
                    if t < NT - 1 or n == 0:
                        mark(ins)
                    else:
                        ins.then_inc(sums_ready, 1)
            split.beside(gi_of(1, l, "v"), 5)
            dve.wait_ge(rstd_ready, job + 2)
            for t in range(NT):
                for n, (a, b) in enumerate(((0, QR), (QR, QR + KVR))):
                    ins = dve.tensor_scalar(c_tok[:, t, a:b], c_tok[:, t, a:b],
                                            rstd[:, 8 + n * NT + t:9 + n * NT + t], None, ALU.mult)
                    if t < NT - 1 or n == 0:
                        mark(ins)
                    else:
                        ins.then_inc(c_scaled, 1)
            split.through(gi_of(1, l, "v"))
            features((1, l, "c"), 3, T, c_hi, c_lo, vec_col(R_C + 3 * l, 3))
            split.through(gi_of(1, l, "uq", 0))
            evict(gi_of(1, l, "uq", 1), lambda b: q[:, b, 4:8, :])
            split.through(gi_of(1, l, "ukv", 0))
            gi = gi_of(1, l, "ukv", 1)
            split.through(gi)
            for b in range(NT):
                wait_gemm_full(dve, gi, b)
                kv = gemm_bank[b][:, :].rearrange("p (h c) -> p h c", h=4)
                mark(dve.tensor_copy(k[:, b, 4:8, 0:NOPE], kv[:, :, 0:NOPE]))
                dve.tensor_copy(v_mla[:, b, 4:8, :], kv[:, :, NOPE:NOPE + MV]).then_inc(gemm_read[b], 1)
            for t in range(NT):
                dve.tensor_copy(k[:, t, :, NOPE:QK], c_tok[:, t, QR + KVR:NC_C].unsqueeze(1)
                                .to_broadcast([P, MH, ROPE])).then_inc(k_rope_ready, 1)
            if l == 0:
                dve.wait_ge(sines_ready, 2)

            def prepare():
                wait_gemm_read(dve, gi_of(1, l, "v"))
                for t in range(NT):
                    mark(dve.bn_stats(stats6[:, t, :], vn[:, t, :]))
                settle()
                for t in range(NT):
                    ins = dve.bn_aggr(mean_var[:, t, :], stats6[:, t, :])
                    if t < NT - 1:
                        mark(ins)
                    else:
                        ins.then_inc(sums_ready, 1)
                yield
                key = (1, l, "sgw", 0)
                bank = aux_wait_full(dve, key)
                view = bank[:, :].rearrange("p (g i) -> p g i", g=4)
                mark(dve.memset(sg_wT[CHUNK:P, :, 0:CHUNK], 0.0))
                mark(dve.tensor_copy(sg_wT[0:CHUNK, :, :], view[0:CHUNK, :, :]))
                dve.tensor_copy(sg_wT[CHUNK:P, :, CHUNK:P], view[CHUNK:P, :, CHUNK:P]).then_inc(read_of(key), 1)
                dve.wait_ge(sg_loaded, 64 * (l + 1))
                dve.wait_ge(rstd_ready, job + 3)
                yield
                for t in range(NT):
                    mark(dve.tensor_scalar(vn[:, t, :], vn[:, t, :], mean_var[:, t, 0:1], rstd[:, t:t + 1],
                                           ALU.subtract, ALU.mult))
                settle()
                yield
                for t in range(NT):
                    mark(dve.tensor_tensor(vn[:, t, :], vn[:, t, :], ln_g[:, :], ALU.mult))
                settle()
                yield
                for t in range(NT):
                    ins = dve.tensor_tensor(vn[:, t, :], vn[:, t, :], ln_b[:, :], ALU.add)
                    if t < NT - 1:
                        mark(ins)
                    else:
                        ins.then_inc(vn_ready, 1)
                yield
                yield from head_norm([q[:, t, :, :] for t in range(NT)] + [k[:, t, :, :] for t in range(NT)])
                for tile, gain in ((q, gain_q), (k, gain_k)):
                    g = gain[:, l, 0:NOPE].unsqueeze(1).to_broadcast([P, MH, NOPE])
                    settle()
                    for t in range(NT):
                        mark(dve.tensor_tensor(tile[:, t, :, 0:NOPE], tile[:, t, :, 0:NOPE], g, ALU.mult))
                        yield
                    yield from rotate(tile, NOPE, HALF, gain[:, l, :], cos1[:, :, :], sin1[:, :, :], table_1, rope_1)
                heads_done()

            def at_end(gi):
                if gi == gi_of(1, l, "za"):
                    wait_gemm_read(dve, gi_of(1, l, "u"))
                    wait_gemm_read(dve, gi_of(1, l, "za"))
                    for g in range(4):
                        mark(dve.tensor_tensor(u[:, g, :], u[:, g, :], za[:, g, :], ALU.mult))

            alongside(prepare(), [gi_of(1, l, n) for n in ("u", "za", "zb")], 2, at_end)
            for g in range(4):
                key = (1, l, "sv", g)
                bank = aux_wait_full(dve, key)
                bias = sg_bias[:, g, :].unsqueeze(1).to_broadcast([P, NT, P])
                dve.tensor_tensor(za[:, g, :].rearrange("p (n i) -> p n i", n=NT),
                                  bank[:, :].rearrange("p (n i) -> p n i", n=NT), bias,
                                  ALU.add).then_inc(read_of(key), 1)
            settle()
            for g in range(4):
                aux_wait_read(dve, (1, l, "sv", g))
                dve.tensor_tensor(u[:, g, :], u[:, g, :], za[:, g, :], ALU.mult).then_inc(ya_ready, 1)
            for g in range(4):
                dve.wait_ge(ya_hi_ready, 4 * l + g + 1)
                dve.tensor_tensor(y_lo[0][:, g, :], u[:, g, :], y_hi[0][:, g, :].bitcast(F32),
                                  ALU.subtract).then_inc(ya_lo_ready, 1)

            def beside_mla(gi):
                dst = {(1, l, "qkc"): lambda b: qk_c[:, b, :], (1, l, "vc"): lambda b: vc[:, b, :]}.get(group_key[gi])
                if dst:
                    evict_now(gi, dst)
                else:
                    wait_gemm_full(dve, gi, 0)
                    dve.tensor_copy(g_T[:, :], gemm_bank[0][0:GR, :]).then_inc(gemm_read[0], 1)

            attention(attention_1(l), beside_mla)
            g_zc = gi_of(1, l, "zc")
            z = zb[:, :, :].rearrange("p t (h d) -> p t h d", h=MH)
            wait_gemm_read(dve, gi_of(1, l, "zb"))
            for t in range(NT):
                dve.tensor_tensor(yb_tok[:, t, :].rearrange("p (h d) -> p h d", h=MH), q[:, t, :, 0:MV],
                                  z[:, t, :, :], ALU.mult).then_inc(rows_gated, 1)
            gates = gla_gates(l)
            next(gates)
            split.beside(g_zc, 0)
            features((1, l, "yb"), 4, T, y_hi[1], y_lo[1])
            alongside(gates, [g_zc], 1)
            gla(l)
            g_00 = [gi_of(1, l, ("gate", 0, 0)), gi_of(1, l, "branch", 0, 0)]
            alongside(gla_rows(l), g_00, 1)
            merge(l, 0, 0)
            merge(l, 0, 1)
            features((1, l, "yc"), 4, T, y_hi[2], y_lo[2])
            merge(l, 0, 2)
            merge(l, 1, 0)
            split_merged(l, 0)
            merge(l, 1, 1)
            merge(l, 1, 2)
            split_merged(l, 1)
            tail(1, l)

        def merge(l, j, i):
            n = 3 * j + i
            g_gate, gi = gi_of(1, l, ("gate", j, i)), gi_of(1, l, "branch", j, i)
            split.through(g_gate)
            split.through(gi)
            settle()
            for m in range(4):
                wait_gemm_read(dve, g_gate, m)
                wait_gemm_full(dve, gi, m)
                mm = merged[:, 4 * j + m, :]
                dst = mm if i == 0 else product[:, m % 2, :]
                if i and m >= 2:
                    settle()
                dve.tensor_tensor(dst, gemm_bank[m][:, :], gate[:, n % 2, m, :], ALU.mult).then_inc(gemm_read[m], 1)
                if i:
                    wait_gemm_read(dve, gi, m)
                    ins = dve.tensor_tensor(mm, mm, product[:, m % 2, :], ALU.add)
                    if i == 2:
                        ins.then_inc(merged_ready, 1)
                    else:
                        mark(ins)

        def split_merged(l, j):
            for m in range(4):
                kk = 4 * j + m
                dve.wait_ge(merged_hi_ready, KD * l + kk + 1)
                dve.tensor_tensor(merged_lo[j][:, m, :], merged[:, kk, :], merged_hi[j][:, m, :].bitcast(F32),
                                  ALU.subtract).then_inc(merged_lo_ready, 1)

        def tail(block, l):
            nxt = next_mem(block, l)
            update_x(block, l, 0)
            if nxt is not None:
                job = 4 * DEPTH + 2 * nxt
                scale_rows(mem_x[nxt], mem_n[nxt], NMEM // P, job + 1, 64, mem_scaled)
            split.beside(gi_of(block, l, "out", 1), 3)
            if nxt is not None:
                features((2, nxt, "mem"), KD, NMEM, mem_hi, mem_lo, vec_col(R_MEM + KD * nxt, KD))
            update_x(block, l, 1)
            if nxt is not None:
                split.through(gi_of(2, nxt, "mkv"))

        def gla_gates(l):
            for m in range(2):
                key = (1, l, "gl", m)
                bank = aux_wait_full(dve, key)
                dve.tensor_scalar(log_a[:, m, :], bank[:, :], vec_col(R_GLA + 2 * l + m), None, ALU.add)\
                   .then_inc(read_of(key), 1)
            for m in range(2):
                aux_wait_read(dve, (1, l, "gl", m))
            dve.scalar_tensor_tensor(out=log_t[:, :, :], in0=log_a[:, :, :], scalar=-1.0, in1=log_a[:, :, :],
                                     op0=ALU.mult, op1=ALU.min).then_inc(gla_gate, 1)
            yield
            yield
            dve.wait_ge(gla_exp, 4 * l + 1)
            mark(dve.scalar_tensor_tensor(out=log_a[:, :, :], in0=log_a[:, :, :], scalar=0.0, in1=log_t[:, :, :],
                                          op0=ALU.min, op1=ALU.subtract))
            dve.wait_ge(gla_loaded, 32 * (l + 1))
            settle()
            mark(dve.tensor_tensor_scan(b_cum[:, 0, :], carry[:, :], log_a[:, 0, :], 0.0, ALU.mult, ALU.add))
            dve.tensor_tensor_scan(b_cum[:, 1, :], carry[:, :], log_a[:, 1, :], 0.0, ALU.mult, ALU.add)\
               .then_inc(gla_gate, 1)
            dve.wait_ge(gla_gate, 3 * l + 2)
            yield
            chunks = b_cum[:, :, :].rearrange("p m (n c) -> p (m n) c", c=CHUNK)
            dve.tensor_tensor(e_st[:, :, :].rearrange("p m (n c) -> p (m n) c", c=CHUNK),
                              chunks[:, :, CHUNK - 1:CHUNK].to_broadcast([P, 2 * T // CHUNK, CHUNK]), chunks,
                              ALU.subtract).then_inc(gla_gate, 1)
            yield
            dve.wait_ge(gla_exp, 4 * l + 2)
            mark(dve.scalar_tensor_tensor(out=qk_c[:, 0:2, :], in0=qk_c[:, 0:2, :], scalar=DK ** -0.5,
                                          in1=e_up[:, :, :], op0=ALU.mult, op1=ALU.mult))
            mark(dve.tensor_copy(decay[:, :, :], e_up[:, :, CHUNK - 1:T:CHUNK]))
            yield
            dve.wait_ge(gla_exp, 4 * l + 3)
            dve.wait_ge(pads_zeroed, 2 * l + 1)
            for hh in range(2):
                r = slice(hh * DK, (hh + 1) * DK)
                ins = dve.tensor_tensor(kt_pad[r, :, hh, :], qk_c[r, 2:4, :], e_dn[r, :, :], ALU.mult)
                if hh:
                    ins.then_inc(gla_qk, 1)
                else:
                    mark(ins)
            yield
            dve.wait_ge(gla_exp, 4 * l + 4)
            dve.wait_ge(gla_qk, 2 * l + 1)
            settle()
            dve.tensor_tensor(qk_c[:, 2:4, :], qk_c[:, 2:4, :], e_st[:, :, :], ALU.mult).then_inc(gla_qk, 1)
            yield

        def gla(l):
            for m in range(2):
                key = (1, l, "ks", m)
                bank = aux_wait_full(dve, key)
                dve.tensor_copy(ks_tok[:, :, m * P:(m + 1) * P], bank[:, :].rearrange("p (t c) -> p t c", t=NT))\
                   .then_inc(read_of(key), 1)
            dve.wait_ge(pads_zeroed, 2 * l + 2)
            for h in range(GH):
                key = (1, l, "att", h)
                bank = aux_wait_full(dve, key)
                dve.copy_predicated(att[:, h, :, :], keep[:, :, :], bank[:, :].rearrange("p (t i) -> p t i", t=NT))\
                   .then_inc(read_of(key), 1)
            for n in range(T // CHUNK - 1):
                key = (1, l, "U", n)
                bank = aux_wait_full(dve, key)
                settle()
                if n:
                    aux_wait_read(dve, (1, l, "U", n - 1))
                for m in range(2):
                    for hh in range(2):
                        r = slice(hh * DK, (hh + 1) * DK)
                        c = slice(hh * DV, (hh + 1) * DV)
                        new = bank[r, m * 2 * DV + hh * DV:m * 2 * DV + (hh + 1) * DV]
                        if n == 0:
                            ins = dve.tensor_copy(state[r, 0, m, c], new)
                        else:
                            ins = dve.scalar_tensor_tensor(out=state[r, n, m, c], in0=state[r, n - 1, m, c],
                                                           scalar=decay[r, m, n:n + 1], in1=new,
                                                           op0=ALU.mult, op1=ALU.add)
                        if m and hh:
                            ins.then_inc(read_of(key), 1)
                        else:
                            mark(ins)

        def gla_rows(l):
            for t in range(NT):
                aux_wait_read(dve, (1, l, "o", t))
                dve.tensor_reduce(sums[:, t * GH:(t + 1) * GH],
                                  o_sq[:, t % 2, :].rearrange("p (h e) -> p h e", h=GH), AX_X, ALU.add)\
                   .then_inc(o_sq_read, 1)
                yield
            dve.wait_ge(o_sq_read, NT * (l + 1))
            dve.engine_nop().then_inc(sums_ready, 1)
            yield
            dve.wait_ge(rstd_ready, 4 * l + 4)
            for t in range(NT):
                r = rstd[:, t * GH:(t + 1) * GH].unsqueeze(2).to_broadcast([P, GH, DV])
                rows = o_tok[:, t, :].rearrange("p (h e) -> p h e", h=GH)
                mark(dve.tensor_tensor(rows, rows, r, ALU.mult))
                yield
            dve.wait_ge(zc_ready, NT * (l + 1))
            settle()
            for t in range(NT):
                dve.tensor_tensor(o_tok[:, t, :], o_tok[:, t, :], zc[:, t, :], ALU.mult).then_inc(rows_gated, 1)
                yield

        def block_2(l):
            job = 4 * DEPTH + 2 * l
            scale_rows(x, x_n[1], NT, job + 2, 0, rows_scaled)
            features((2, l, "x"), KD, T, act_hi, act_lo, vec_col(R_X + KD * (DEPTH + l), KD))
            split.through(gi_of(2, l, "aq"))
            evict(gi_of(2, l, "ak"), lambda b: flat_2("ak")[:, b, :])

            def kind_heads(a, gain):
                qq, kk = kinds[a + "q"], kinds[a + "k"]
                yield from head_norm([tile[:, t, :, :] for tile in (qq, kk) for t in range(NT)])
                for tile, g in ((qq, gain), (kk, gain + 1)):
                    yield from rotate(tile, 0, HD // 2, gain_2[:, l, g, :], cos2[:, :, :], sin2[:, :, :],
                                      table_2, rope_2)
                heads_done()

            def memory_heads():
                tiles = ([m_tok[:, t, 0, :, :] for t in range(NT)] + [mkv[:, t, 0, :, :] for t in range(NMEM // P)])
                yield from head_norm(tiles)
                settle()
                for n, tile in enumerate(tiles):
                    g = gain_2[:, l, 4 if n < NT else 5, :].unsqueeze(1).to_broadcast([P, EH, HD])
                    mark(dve.tensor_tensor(tile, tile, g, ALU.mult))
                    yield
                heads_done()

            def beside_2(gi):
                evict_now(gi, lambda b: flat_2(group_key[gi][2])[:, b, :])

            def twice(work):
                return lambda n: [next(work, None), next(work, None)]

            def at_end(gi):
                if gi == gi_of(2, l, "bq"):
                    evict_now(gi, lambda b: flat_2("bq")[:, b, :])

            dve.wait_ge(keys_zeroed, 1)
            alongside(kind_heads("a", 0), [gi_of(2, l, n) for n in ("av", "bq", "bk")], 2, at_end)
            b_heads = kind_heads("b", 2)
            attention(attention_2(l, "moba"), beside_2, twice(b_heads))
            for _ in b_heads:
                pass
            m_heads = memory_heads()
            attention(attention_2(l, "dilated"), None, twice(m_heads))
            for _ in m_heads:
                pass

            def gated(y, g, c0, width, ts=range(NT)):
                for t in ts:
                    rows = flat_2(y)[:, t, 0:width]
                    dve.tensor_tensor(rows, rows, flat_2(g)[:, t, c0:c0 + width], ALU.mult).then_inc(rows_gated, 1)

            wait_gemm_read(dve, gi_of(2, l, "ag"))
            gated("aq", "ag", 0, WA)
            wait_gemm_read(dve, gi_of(2, l, "bg"))

            def y_parts(n):
                if n in (1, 2):
                    gated("bq", "bg", 0, WB, range(2 * n - 2, 2 * n))
                if n < TURNS_FIRST:
                    name, kk = ("aq", n) if n < 3 else ("bq", n - 3)
                    hi_count[0] += 1
                    dve.wait_ge(feat_hi_ready, hi_count[0])
                    key = (2, l, "y" + name, kk)
                    dve.tensor_tensor(act_lo[:, n, :], aux_bank[aux_place[key][0]][:, :],
                                      act_hi[:, n, :].bitcast(F32), ALU.subtract).then_inc(read_of(key), 1)

            attention(attention_2(l, "memory"), None, y_parts, True)
            dve.wait_ge(silu_ready, l + 1)
            gated("m", "m", WE, WE)
            features((2, l, "ym"), 2, T, act_hi, act_lo, None, 6)
            tail(2, l)

        dve.wait_ge(consts_loaded, 16 * N_CONST)
        dve.tensor_copy(vec_rows[R_POS:R_POS + NT, :], pos_rows[R_POS:R_POS + NT, :]).then_inc(positions_ready, 1)
        bank = aux_wait_full(dve, "vec")
        dve.tensor_copy(vec_cols[:, :], bank[:, 0:N_ROWS]).then_inc(read_of("vec"), 1)
        aux_wait_read(dve, "vec")
        for l in range(DEPTH):
            block_1(l)
        for l in range(DEPTH):
            block_2(l)

    @block.gpsimd
    def _(pool):
        marks = [0]

        def mark(ins):
            ins.then_inc(pool_done, 1)
            marks[0] += 1

        def factors(source, c0, n, scale):
            mark(pool.tensor_scalar(mean_sq[:, c0:c0 + n], source, scale, EPS, ALU.mult, ALU.add))
            pool.wait_ge(pool_done, marks[0])
            pool.tensor_tensor(rstd[:, c0:c0 + n], mean_sq[:, c0:c0 + n], minus_half[:, 0:n], ALU.pow)\
                .then_inc(rstd_ready, 1)

        def factors_x(count):
            pool.wait_ge(squares_ready, count)
            mark(pool.tensor_tensor(mean_sq[:, NT:2 * NT], sums[:, 0:NT], sums[:, NT:2 * NT], ALU.add))
            pool.wait_ge(pool_done, marks[0])
            factors(mean_sq[:, NT:2 * NT], 0, NT, 1.0)

        mark(pool.memset(minus_half[:, :], -0.5))
        pool.wait_ge(pool_done, marks[0])
        for l in range(DEPTH):
            factors_x(2 * NT * (l + 1))
            pool.wait_ge(sums_ready, 3 * l + 1)
            factors(sums[:, 8:8 + 2 * NT], 8, 2 * NT, 1.0)
            pool.wait_ge(sums_ready, 3 * l + 2)
            factors(mean_var[:, :, 1], 0, NT, 1.0)
            pool.wait_ge(rows_gated, NT * (2 * l + 1))
            pool.memset(kt_pad[:, :, :, :], 0.0).then_inc(pads_zeroed, 1)
            pool.wait_ge(gla_qk, 2 * l + 2)
            mark(pool.memset(att[:, :, :, :], 0.0))
            pool.memset(state[:, :, :, :], 0.0).then_inc(pads_zeroed, 1)
            wait_gemm_read(pool, gi_of(1, l, "zc"))
            for t in range(NT):
                rows = zc[:, t, :].rearrange("p (h e) -> p h e", h=GH)
                pool.tensor_tensor(rows, rows, gain_o[:, l, :].unsqueeze(1).to_broadcast([P, GH, DV]), ALU.mult)\
                    .then_inc(zc_ready, 1)
            pool.wait_ge(sums_ready, 3 * l + 3)
            factors(sums[:, 0:NT * GH], 0, NT * GH, 1.0 / DV)
        for l in range(DEPTH):
            before = 2 * NT * DEPTH + (2 * NT + NMEM // P) * l
            pool.wait_ge(squares_ready, before + NMEM // P)
            factors(sums[:, 64:64 + NMEM // P], 64, NMEM // P, 1.0)
            if l == 0:
                aux_wait_full(pool, (2, 0, "mem", KD - 1))
                pool.memset(kT_2[:, :, :, :], 0.0).then_inc(keys_zeroed, 1)
            factors_x(before + NMEM // P + 2 * NT)

    @block.sync
    def _(sp):
        def load_piece(p):
            gi, k0, k1 = pieces[p]
            g = groups[gi]
            if p >= RAW:
                old_gi, _, old_k1 = pieces[p - RAW]
                sp.wait_ge(w_lo_ready, first_step[old_gi] + old_k1)
            sp.dma_start(raw[:, p % RAW, 0:k1 - k0, 0:g.n], g.src(k0, k1).rearrange("(k p) n -> p k n", p=P))\
              .then_inc(raw_loaded[p % RAW], 16)

        sp.dma_start(x[:, :, :], w["x"][0].rearrange("(t p) d -> p t d", p=P)).then_inc(x_loaded, 16)
        for dst, src in const_loads:
            sp.dma_start(dst, src).then_inc(consts_loaded, 16)
        for p in range(len(pieces)):
            load_piece(p)
        for j in range(2):
            wait_gemm_read(sp, gi_of(2, DEPTH - 1, "out", j))
            sp.dma_start(out[0].rearrange("(t p) d -> p t d", p=P)[:, :, j * T:(j + 1) * T],
                         x[:, :, j * T:(j + 1) * T]).then_inc(out_stored, 16)
        sp.wait_ge(out_stored, 32)


_INS = ["x", "positions", "norm_g", "w_in", "b_gate", "sg_ln_g", "sg_ln_b", "sg_w", "sg_b", "mla_cq_g", "mla_ckv_g",
        "mla_w_uq", "mla_w_ukv", "mla_q_g", "mla_k_g", "gla_w_gate", "gla_b_gate", "gla_o_g", "w_branch", "w_out",
        "mem_2", "norm_g_2", "w_in_2", "w_out_2", "mem_norm_g_2", "w_mem_kv_2", "qk_g_2"]


def kernel(**inputs):
    import concourse.bacc as bacc
    from concourse.bass_utils import run_bass_kernel_spmd

    nc = bacc.Bacc("TRN2", target_bir_lowering=False, num_devices=1)
    given = {name: np.ascontiguousarray(inputs[name]) for name in _INS}
    given.update(constants())
    w = {name: nc.dram_tensor(f"in_{name}", a.shape, mybir.dt.from_np(a.dtype), kind="ExternalInput").ap()
         for name, a in given.items()}
    out = nc.dram_tensor("out_x", (1, T, D), F32, kind="ExternalOutput").ap()
    with ExitStack() as stack:
        hybrid_kernel(nc, w, out, stack)
    r = run_bass_kernel_spmd(nc, [{f"in_{name}": a for name, a in given.items()}], core_ids=[0])
    return r.results[0]["out_x"]
```
